# Optimizing a Trainium2 kernel written in Bass

```python
import math
import jax, jax.numpy as jnp
from jax import lax
import numpy as np

D_MODEL = 1024
BATCH = 1
SEQ = 512
DEPTH = 2

HEAD_DIM = 64
SCALE = HEAD_DIM ** -0.5
ROPE_THETA = 10000.0
NORM_EPS = 1e-5
BAND = 128

A_HEADS = 8
A_KV_HEADS = 2
A_GROUP = A_HEADS // A_KV_HEADS
CMP_BLOCK = 32
CMP_STRIDE = 16
CMP_HIDDEN = 256
SEL_BLOCK = 64
SEL_TOPK = 16
NSA_WINDOW = 512
NSA_QBLOCK = 64
N_BRANCH = 3

B_HEADS = 8
B_KV_HEADS = 2
B_GROUP = B_HEADS // B_KV_HEADS
B_WINDOW = 128

C_HEADS = 16
C_PATTERNS = ((128, 1), (512, 4), (2048, 16))

A_Q = A_HEADS * HEAD_DIM
A_KV = A_KV_HEADS * HEAD_DIM
A_GATES = A_HEADS * N_BRANCH
B_Q = B_HEADS * HEAD_DIM
B_KV = B_KV_HEADS * HEAD_DIM
EVEN_IN = A_Q + 6 * A_KV + A_GATES + B_Q + 2 * B_KV
EVEN_MIX = A_Q + B_Q
ODD_IN = 3 * C_HEADS * HEAD_DIM
ODD_MIX = C_HEADS * HEAD_DIM
FFN_HIDDEN = -(-8 * D_MODEL // (3 * 256)) * 256
N_EVEN = (DEPTH + 1) // 2
N_ODD = DEPTH // 2


def rms_norm(x, g):
    xf = x.astype(jnp.float32)
    y = xf * lax.rsqrt(jnp.mean(xf * xf, axis=-1, keepdims=True) + NORM_EPS)
    return (y * g.astype(jnp.float32)).astype(x.dtype)

def rope_tables(seq, dtype):
    inv = 1.0 / (ROPE_THETA ** (jnp.arange(0, HEAD_DIM, 2, dtype=jnp.float32) / HEAD_DIM))
    ang = jnp.arange(seq, dtype=jnp.float32)[:, None] * inv[None, :]
    ang = jnp.concatenate([ang, ang], axis=-1)
    return jnp.cos(ang).astype(dtype), jnp.sin(ang).astype(dtype)

def apply_rope(x, cos, sin):
    x1, x2 = jnp.split(x, 2, axis=-1)
    rot = jnp.concatenate([-x2, x1], axis=-1)
    return x * cos[:, None, :] + rot * sin[:, None, :]

def banded_attention(q, k, v, reach, sink=None):
    L, dh = q.shape[-2], q.shape[-1]
    nb = -(-L // BAND)
    pad = nb * BAND - L
    if pad:
        q = jnp.pad(q, [(0, 0)] * (q.ndim - 2) + [(0, pad), (0, 0)])
        k = jnp.pad(k, [(0, 0)] * (k.ndim - 2) + [(0, pad), (0, 0)])
        v = jnp.pad(v, [(0, 0)] * (v.ndim - 2) + [(0, pad), (0, 0)])
    qb = q.reshape(q.shape[:-2] + (nb, BAND, dh))
    kb = k.reshape(k.shape[:-2] + (nb, BAND, dh))
    vb = v.reshape(v.shape[:-2] + (nb, BAND, dh))

    def with_prev(t):
        prev = jnp.pad(t, [(0, 0)] * (t.ndim - 3) + [(1, 0), (0, 0), (0, 0)])[..., :-1, :, :]
        return jnp.concatenate([prev, t], axis=-2)

    kc, vc = with_prev(kb), with_prev(vb)
    s = jnp.einsum('...gnqd,...nkd->...gnqk', qb, kc, preferred_element_type=jnp.float32) * SCALE
    qi = jnp.arange(BAND)[:, None] + BAND
    kj = jnp.arange(2 * BAND)[None, :]
    diff = qi - kj
    mask = (diff >= 0) & (diff <= reach)
    not_before_start = (jnp.arange(nb)[:, None, None] > 0) | (kj[None] >= BAND)
    mask = mask[None] & not_before_start
    s = jnp.where(mask, s, -jnp.inf)
    m = jnp.max(s, axis=-1)
    if sink is not None:
        m = jnp.maximum(m, sink)
    p = jnp.exp(s - m[..., None])
    den = jnp.sum(p, axis=-1)
    if sink is not None:
        den = den + jnp.exp(sink - m)
    o = jnp.einsum('...gnqk,...nkd->...gnqd', p, vc.astype(jnp.float32)) / den[..., None]
    o = o.reshape(q.shape[:-2] + (nb * BAND, dh))[..., :L, :]
    lse = (m + jnp.log(den)).reshape(q.shape[:-2] + (nb * BAND,))[..., :L]
    return o, lse

def compress_blocks(t, pe, w1, w2):
    bsz, hkv, seq, dh = t.shape
    chunks = t.reshape(bsz, hkv, seq // CMP_STRIDE, CMP_STRIDE, dh)
    blocks = jnp.concatenate([chunks[:, :, :-1], chunks[:, :, 1:]], axis=-2)
    nc = blocks.shape[2]
    blocks = (blocks + pe).reshape(bsz, hkv, nc, CMP_BLOCK * dh)
    return jax.nn.silu(blocks @ w1) @ w2

def nsa_attention(q_plain, q_rot, k_cmp, v_cmp, k_sel, v_sel, k_win, v_win, gates,
                  pe_k, pe_v, wk1, wk2, wv1, wv2):
    bsz, seq = q_plain.shape[:2]
    dh = HEAD_DIM
    nc = seq // CMP_STRIDE - 1
    nb = seq // SEL_BLOCK
    n_sel = min(SEL_TOPK, nb)

    def group_q(t):
        return t.reshape(bsz, seq, A_KV_HEADS, A_GROUP, dh).transpose(0, 2, 3, 1, 4)

    def heads_first(t):
        return t.transpose(0, 2, 1, 3)

    qp, qr = group_q(q_plain), group_q(q_rot)
    g = gates.reshape(bsz, seq, A_KV_HEADS, A_GROUP, N_BRANCH).transpose(0, 2, 3, 1, 4)
    kc = compress_blocks(heads_first(k_cmp), pe_k, wk1, wk2)
    vc = compress_blocks(heads_first(v_cmp), pe_v, wv1, wv2).astype(jnp.float32)
    ks_b = heads_first(k_sel).reshape(bsz, A_KV_HEADS, nb, SEL_BLOCK, dh)
    vs_b = heads_first(v_sel).reshape(bsz, A_KV_HEADS, nb, SEL_BLOCK, dh)
    pad_w = ((0, 0), (0, 0), (NSA_WINDOW, 0), (0, 0))
    kw_p = jnp.pad(heads_first(k_win), pad_w)
    vw_p = jnp.pad(heads_first(v_win), pad_w)

    cmp_end = jnp.arange(nc) * CMP_STRIDE + CMP_BLOCK - 1
    c_start = np.arange(nc) * CMP_STRIDE
    s_start = np.arange(nb) * SEL_BLOCK
    overlap = ((c_start[:, None] <= s_start[None, :] + SEL_BLOCK - 1) &
               (c_start[:, None] + CMP_BLOCK - 1 >= s_start[None, :]))
    cmp_to_sel = jnp.asarray(overlap.astype(np.float32))
    bi = jnp.arange(bsz)[:, None, None, None]
    hi = jnp.arange(A_KV_HEADS)[None, :, None, None]
    blk = jnp.arange(nb)[None, :]

    def query_block(i):
        q0 = i * NSA_QBLOCK
        tq = q0 + jnp.arange(NSA_QBLOCK)
        qp_b = lax.dynamic_slice_in_dim(qp, q0, NSA_QBLOCK, axis=3)
        qr_b = lax.dynamic_slice_in_dim(qr, q0, NSA_QBLOCK, axis=3)
        g_b = lax.dynamic_slice_in_dim(g, q0, NSA_QBLOCK, axis=3).astype(jnp.float32)

        s = jnp.einsum('bhgqd,bhcd->bhgqc', qp_b, kc, preferred_element_type=jnp.float32) * SCALE
        s = jnp.where(cmp_end[None, :] <= tq[:, None], s, -jnp.inf)
        m = jnp.max(s, axis=-1, keepdims=True)
        m = jnp.where(jnp.isfinite(m), m, 0.0)
        p = jnp.exp(s - m)
        den = jnp.sum(p, axis=-1, keepdims=True)
        p = p / jnp.where(den > 0, den, 1.0)
        o_cmp = jnp.einsum('bhgqc,bhcd->bhgqd', p, vc)

        imp = jnp.einsum('bhgqc,cn->bhqn', p, cmp_to_sel)
        cur = (tq // SEL_BLOCK)[:, None]
        forced = (blk == 0) | (blk == cur) | (blk == cur - 1)
        imp = jnp.where(forced, jnp.inf, jnp.where(blk > cur, -jnp.inf, imp))
        _, idx = lax.top_k(imp, n_sel)
        kg = ks_b[bi, hi, idx].reshape(bsz, A_KV_HEADS, NSA_QBLOCK, n_sel * SEL_BLOCK, dh)
        vg = vs_b[bi, hi, idx].reshape(bsz, A_KV_HEADS, NSA_QBLOCK, n_sel * SEL_BLOCK, dh)
        pos = (idx[..., None] * SEL_BLOCK + jnp.arange(SEL_BLOCK)).reshape(
            bsz, A_KV_HEADS, NSA_QBLOCK, n_sel * SEL_BLOCK)
        s = jnp.einsum('bhgqd,bhqkd->bhgqk', qr_b, kg, preferred_element_type=jnp.float32) * SCALE
        s = jnp.where((pos <= tq[:, None])[:, :, None], s, -jnp.inf)
        o_sel = jnp.einsum('bhgqk,bhqkd->bhgqd', jax.nn.softmax(s, axis=-1), vg.astype(jnp.float32))

        kw = lax.dynamic_slice_in_dim(kw_p, q0, NSA_QBLOCK + NSA_WINDOW, axis=2)
        vw = lax.dynamic_slice_in_dim(vw_p, q0, NSA_QBLOCK + NSA_WINDOW, axis=2)
        kpos = q0 - NSA_WINDOW + jnp.arange(NSA_QBLOCK + NSA_WINDOW)
        diff = tq[:, None] - kpos[None, :]
        wmask = (diff >= 0) & (diff < NSA_WINDOW) & (kpos[None, :] >= 0)
        s = jnp.einsum('bhgqd,bhkd->bhgqk', qr_b, kw, preferred_element_type=jnp.float32) * SCALE
        s = jnp.where(wmask, s, -jnp.inf)
        o_win = jnp.einsum('bhgqk,bhkd->bhgqd', jax.nn.softmax(s, axis=-1), vw.astype(jnp.float32))

        return g_b[..., 0:1] * o_cmp + g_b[..., 1:2] * o_sel + g_b[..., 2:3] * o_win

    out = lax.map(query_block, jnp.arange(seq // NSA_QBLOCK))
    out = out.transpose(1, 0, 4, 2, 3, 5)
    return out.reshape(bsz, seq, A_HEADS * dh)

def swa_sink_attention(q, k, v, sinks):
    bsz, seq = q.shape[:2]
    qg = q.reshape(bsz, seq, B_KV_HEADS, B_GROUP, HEAD_DIM).transpose(0, 2, 3, 1, 4)
    sink = sinks.astype(jnp.float32).reshape(B_KV_HEADS, B_GROUP, 1, 1)
    o, _ = banded_attention(qg, k.transpose(0, 2, 1, 3), v.transpose(0, 2, 1, 3), B_WINDOW - 1, sink)
    return o.transpose(0, 3, 1, 2, 4).reshape(bsz, seq, B_HEADS * HEAD_DIM)

def dilated_attention(q, k, v):
    bsz, seq, nh, dh = q.shape
    qt, kt, vt = (t.transpose(0, 2, 1, 3) for t in (q, k, v))
    outs, lses = [], []
    for window, dil in C_PATTERNS:
        sub = seq // dil

        def strided(t):
            return t.reshape(bsz, nh, sub, dil, dh).transpose(0, 1, 3, 2, 4)

        o, lse = banded_attention(strided(qt)[..., None, :, :], strided(kt), strided(vt), window // dil)
        outs.append(o[..., 0, :, :].transpose(0, 1, 3, 2, 4).reshape(bsz, nh, seq, dh))
        lses.append(lse[..., 0, :].transpose(0, 1, 3, 2).reshape(bsz, nh, seq))
    w = jax.nn.softmax(jnp.stack(lses, axis=0), axis=0)
    o = jnp.einsum('pbht,pbhtd->bhtd', w, jnp.stack(outs, axis=0))
    return o.transpose(0, 2, 1, 3).reshape(bsz, seq, nh * dh)

def first_inputs(seed: int = 0) -> dict:
    key = jax.random.key(seed)
    ks = jax.random.split(key, 17)
    nrm = jax.random.normal
    f32 = jnp.float32
    return {
        "x": nrm(ks[0], (BATCH, SEQ, D_MODEL), f32),
        "attn_norm": 1.0 + 0.02 * nrm(ks[1], (DEPTH, D_MODEL), f32),
        "ffn_norm": 1.0 + 0.02 * nrm(ks[2], (DEPTH, D_MODEL), f32),
        "final_norm": 1.0 + 0.02 * nrm(ks[3], (D_MODEL,), f32),
        "w_in_e": nrm(ks[4], (N_EVEN, D_MODEL, EVEN_IN), f32) * D_MODEL ** -0.5,
        "w_out_e": nrm(ks[5], (N_EVEN, EVEN_MIX, D_MODEL), f32) * EVEN_MIX ** -0.5,
        "cmp_pe_k": 0.02 * nrm(ks[6], (N_EVEN, CMP_BLOCK, HEAD_DIM), f32),
        "cmp_pe_v": 0.02 * nrm(ks[7], (N_EVEN, CMP_BLOCK, HEAD_DIM), f32),
        "cmp_k_w1": nrm(ks[8], (N_EVEN, CMP_BLOCK * HEAD_DIM, CMP_HIDDEN), f32) * (CMP_BLOCK * HEAD_DIM) ** -0.5,
        "cmp_k_w2": nrm(ks[9], (N_EVEN, CMP_HIDDEN, HEAD_DIM), f32) * CMP_HIDDEN ** -0.5,
        "cmp_v_w1": nrm(ks[10], (N_EVEN, CMP_BLOCK * HEAD_DIM, CMP_HIDDEN), f32) * (CMP_BLOCK * HEAD_DIM) ** -0.5,
        "cmp_v_w2": nrm(ks[11], (N_EVEN, CMP_HIDDEN, HEAD_DIM), f32) * CMP_HIDDEN ** -0.5,
        "sinks": 0.5 * nrm(ks[12], (N_EVEN, B_HEADS), f32),
        "w_qkv_o": nrm(ks[13], (N_ODD, D_MODEL, ODD_IN), f32) * D_MODEL ** -0.5,
        "w_out_o": nrm(ks[14], (N_ODD, ODD_MIX, D_MODEL), f32) * ODD_MIX ** -0.5,
        "w_gate_up": nrm(ks[15], (DEPTH, D_MODEL, 2 * FFN_HIDDEN), f32) * D_MODEL ** -0.5,
        "w_down": nrm(ks[16], (DEPTH, FFN_HIDDEN, D_MODEL), f32) * FFN_HIDDEN ** -0.5,
    }

def first_block(x, attn_norm, ffn_norm, final_norm, w_in_e, w_out_e, cmp_pe_k, cmp_pe_v,
              cmp_k_w1, cmp_k_w2, cmp_v_w1, cmp_v_w2, sinks, w_qkv_o, w_out_o,
              w_gate_up, w_down):
    bsz, seq, _ = x.shape
    cos, sin = rope_tables(seq, x.dtype)
    for layer in range(DEPTH):
        h = rms_norm(x, attn_norm[layer])
        if layer % 2 == 0:
            i = layer // 2
            z = h @ w_in_e[i]
            o1 = A_Q
            o2 = o1 + 6 * A_KV
            o3 = o2 + A_GATES
            o4 = o3 + B_Q
            aq = z[..., :o1].reshape(bsz, seq, A_HEADS, HEAD_DIM)
            akc, avc, aks, avs, akw, avw = [t.reshape(bsz, seq, A_KV_HEADS, HEAD_DIM)
                                            for t in jnp.split(z[..., o1:o2], 6, axis=-1)]
            gates = jax.nn.sigmoid(z[..., o2:o3].astype(jnp.float32)).reshape(bsz, seq, A_HEADS, N_BRANCH)
            bq = apply_rope(z[..., o3:o4].reshape(bsz, seq, B_HEADS, HEAD_DIM), cos, sin)
            bk, bv = [t.reshape(bsz, seq, B_KV_HEADS, HEAD_DIM) for t in jnp.split(z[..., o4:], 2, axis=-1)]
            bk = apply_rope(bk, cos, sin)
            a_out = nsa_attention(aq, apply_rope(aq, cos, sin), akc, avc,
                                  apply_rope(aks, cos, sin), avs, apply_rope(akw, cos, sin), avw, gates,
                                  cmp_pe_k[i], cmp_pe_v[i], cmp_k_w1[i], cmp_k_w2[i], cmp_v_w1[i], cmp_v_w2[i])
            b_out = swa_sink_attention(bq, bk, bv, sinks[i])
            mix = jnp.concatenate([a_out, b_out], axis=-1).astype(x.dtype)
            x = x + mix @ w_out_e[i]
        else:
            j = layer // 2
            z = h @ w_qkv_o[j]
            q, k, v = [t.reshape(bsz, seq, C_HEADS, HEAD_DIM) for t in jnp.split(z, 3, axis=-1)]
            c_out = dilated_attention(apply_rope(q, cos, sin), apply_rope(k, cos, sin), v)
            x = x + c_out.astype(x.dtype) @ w_out_o[j]
        h = rms_norm(x, ffn_norm[layer])
        gate, up = jnp.split(h @ w_gate_up[layer], 2, axis=-1)
        x = x + (jax.nn.silu(gate) * up) @ w_down[layer]
    return rms_norm(x, final_norm)


N_EVEN_2 = (DEPTH + 1) // 2
N_ODD_2 = DEPTH // 2
EPS = 1e-6
NEG_INF = -1e30
Q_BLOCK = 128
FOX_WIDTH = D_MODEL // 2
FOX_HEAD_DIM = 64
FOX_HEADS = FOX_WIDTH // FOX_HEAD_DIM
SC_WIDTH = D_MODEL - FOX_WIDTH
SC_GROUPS = SC_WIDTH // 64
SC_K = 3
AB_IN = 3 * FOX_WIDTH + FOX_HEADS + 3 * SC_WIDTH
LRU_WIDTH = D_MODEL
LRU_BW = 256
LRU_BLOCKS = LRU_WIDTH // LRU_BW
RG_CONV_K = 4
RG_C = 8.0
RG_MIN_RAD = 0.9
RG_MAX_RAD = 0.999
MEM_LEN = 256
MEM_HEADS = 4
MEM_HEAD_DIM = D_MODEL // MEM_HEADS
D_FF = ((8 * D_MODEL // 3 + 255) // 256) * 256


def rmsnorm(x, g):
    x32 = x.astype(jnp.float32)
    y = x32 * lax.rsqrt(jnp.mean(x32 * x32, axis=-1, keepdims=True) + EPS)
    return y.astype(x.dtype) * g

def causal_depthwise_conv(x, w):
    k_width, ch = w.shape
    return lax.conv_general_dilated(
        x, w[:, None, :], window_strides=(1,), padding=[(k_width - 1, 0)],
        dimension_numbers=("NWC", "WIO", "NWC"), feature_group_count=ch)

def forgetting_attention(q, k, v, log_f):
    seq = q.shape[1]
    scale = q.shape[-1] ** -0.5
    cum = jnp.cumsum(log_f, axis=1).transpose(0, 2, 1)
    outs = []
    for blk in range(seq // Q_BLOCK):
        lo, hi = blk * Q_BLOCK, (blk + 1) * Q_BLOCK
        s = jnp.einsum("bqhd,bkhd->bhqk", q[:, lo:hi], k[:, :hi],
                       preferred_element_type=jnp.float32) * scale
        s = s + cum[:, :, lo:hi, None] - cum[:, :, None, :hi]
        causal = (lo + jnp.arange(Q_BLOCK))[:, None] >= jnp.arange(hi)[None, :]
        s = jnp.where(causal, s, NEG_INF)
        p = jax.nn.softmax(s, axis=-1).astype(v.dtype)
        outs.append(jnp.einsum("bhqk,bkhd->bqhd", p, v[:, :hi]))
    return jnp.concatenate(outs, axis=1)

def fox_shortconv_mixer(h, w_in, b_f, conv_w, w_out):
    bsz, seq, _ = h.shape
    proj = h @ w_in
    i1 = FOX_WIDTH
    i2 = 2 * FOX_WIDTH
    i3 = 3 * FOX_WIDTH
    i4 = i3 + FOX_HEADS
    i5 = i4 + SC_WIDTH
    i6 = i5 + SC_WIDTH
    q, k, v, f_logit, b_gate, c_gate, u = jnp.split(proj, [i1, i2, i3, i4, i5, i6], axis=-1)
    heads = lambda t: t.reshape(bsz, seq, FOX_HEADS, FOX_HEAD_DIM)
    log_f = jax.nn.log_sigmoid((f_logit + b_f).astype(jnp.float32))
    y_a = forgetting_attention(heads(q), heads(k), heads(v), log_f).reshape(bsz, seq, FOX_WIDTH)
    y_b = b_gate * causal_depthwise_conv(c_gate * u, conv_w)
    return jnp.concatenate([y_a, y_b], axis=-1) @ w_out

def _lru_combine(c1, c2):
    a1, b1 = c1
    a2, b2 = c2
    return a1 * a2, a2 * b1 + b2

def rglru_mixer(h, w_in, conv_w, conv_b, w_a, b_a, w_i, b_i, lam, w_out):
    bsz, seq, _ = h.shape
    gate, u = jnp.split(h @ w_in, 2, axis=-1)
    u = causal_depthwise_conv(u, conv_w) + conv_b
    ub = u.reshape(bsz, seq, LRU_BLOCKS, LRU_BW)
    r = jax.nn.sigmoid(jnp.einsum("bsnc,ncd->bsnd", ub, w_a) + b_a).reshape(bsz, seq, LRU_WIDTH)
    i = jax.nn.sigmoid(jnp.einsum("bsnc,ncd->bsnd", ub, w_i) + b_i).reshape(bsz, seq, LRU_WIDTH)
    log_a = -RG_C * r.astype(jnp.float32) * jax.nn.softplus(-lam.astype(jnp.float32))
    a = jnp.exp(log_a)
    b = jnp.sqrt(-jnp.expm1(2.0 * log_a)) * (i * u).astype(jnp.float32)
    _, hs = lax.associative_scan(_lru_combine, (a, b), axis=1)
    y = jax.nn.gelu(gate) * hs.astype(h.dtype)
    return y @ w_out

def memory_cross_attention(h, m, w_q, w_kv, w_o):
    bsz, seq, _ = h.shape
    mlen = m.shape[1]
    q = (h @ w_q).reshape(bsz, seq, MEM_HEADS, MEM_HEAD_DIM)
    k, v = jnp.split(m @ w_kv, 2, axis=-1)
    k = k.reshape(bsz, mlen, MEM_HEADS, MEM_HEAD_DIM)
    v = v.reshape(bsz, mlen, MEM_HEADS, MEM_HEAD_DIM)
    s = jnp.einsum("bqhd,bkhd->bhqk", q, k, preferred_element_type=jnp.float32) * (MEM_HEAD_DIM ** -0.5)
    p = jax.nn.softmax(s, axis=-1).astype(v.dtype)
    o = jnp.einsum("bhqk,bkhd->bqhd", p, v).reshape(bsz, seq, D_MODEL)
    return o @ w_o

def swiglu(h, w_gu, w_down):
    g, u = jnp.split(h @ w_gu, 2, axis=-1)
    return (jax.nn.silu(g) * u) @ w_down

def second_inputs(seed: int = 0) -> dict:
    key = jax.random.key(seed)
    ks = iter(jax.random.split(key, 40))
    dense = lambda shape, fan_in: jax.random.normal(next(ks), shape, jnp.float32) * (fan_in ** -0.5)
    gain = lambda shape: 1.0 + 0.02 * jax.random.normal(next(ks), shape, jnp.float32)
    small = lambda shape: 0.01 * jax.random.normal(next(ks), shape, jnp.float32)
    x = jax.random.normal(next(ks), (BATCH, SEQ, D_MODEL), jnp.float32)
    mem = jax.random.normal(next(ks), (BATCH, MEM_LEN, D_MODEL), jnp.float32)
    rad = jax.random.uniform(next(ks), (N_ODD_2, LRU_WIDTH), jnp.float32, RG_MIN_RAD, RG_MAX_RAD)
    c_lam = -jnp.log(jnp.expm1(-jnp.log(rad) / RG_C))
    return {
        "x": x,
        "mem": mem,
        "g_mix_pre": gain((DEPTH, D_MODEL)),
        "g_mix_post": gain((DEPTH, D_MODEL)),
        "g_cross_pre": gain((DEPTH, D_MODEL)),
        "g_mem": gain((DEPTH, D_MODEL)),
        "g_cross_post": gain((DEPTH, D_MODEL)),
        "g_ffn_pre": gain((DEPTH, D_MODEL)),
        "g_ffn_post": gain((DEPTH, D_MODEL)),
        "w_xq": dense((DEPTH, D_MODEL, D_MODEL), D_MODEL),
        "w_xkv": dense((DEPTH, D_MODEL, 2 * D_MODEL), D_MODEL),
        "w_xo": dense((DEPTH, D_MODEL, D_MODEL), D_MODEL),
        "w_ffn_gu": dense((DEPTH, D_MODEL, 2 * D_FF), D_MODEL),
        "w_ffn_down": dense((DEPTH, D_FF, D_MODEL), D_FF),
        "ab_w_in": dense((N_EVEN_2, D_MODEL, AB_IN), D_MODEL),
        "ab_b_f": jax.random.uniform(next(ks), (N_EVEN_2, FOX_HEADS), jnp.float32, 2.0, 5.0),
        "ab_conv_w": dense((N_EVEN_2, SC_K, SC_WIDTH), SC_K),
        "ab_w_out": dense((N_EVEN_2, D_MODEL, D_MODEL), D_MODEL),
        "c_w_in": dense((N_ODD_2, D_MODEL, 2 * LRU_WIDTH), D_MODEL),
        "c_conv_w": dense((N_ODD_2, RG_CONV_K, LRU_WIDTH), RG_CONV_K),
        "c_conv_b": small((N_ODD_2, LRU_WIDTH)),
        "c_w_a": dense((N_ODD_2, LRU_BLOCKS, LRU_BW, LRU_BW), LRU_BW),
        "c_b_a": small((N_ODD_2, LRU_BLOCKS, LRU_BW)),
        "c_w_i": dense((N_ODD_2, LRU_BLOCKS, LRU_BW, LRU_BW), LRU_BW),
        "c_b_i": small((N_ODD_2, LRU_BLOCKS, LRU_BW)),
        "c_lam": c_lam,
        "c_w_out": dense((N_ODD_2, LRU_WIDTH, D_MODEL), LRU_WIDTH),
    }

def second_block(x, mem, g_mix_pre, g_mix_post, g_cross_pre, g_mem, g_cross_post,
              g_ffn_pre, g_ffn_post, w_xq, w_xkv, w_xo, w_ffn_gu, w_ffn_down,
              ab_w_in, ab_b_f, ab_conv_w, ab_w_out,
              c_w_in, c_conv_w, c_conv_b, c_w_a, c_b_a, c_w_i, c_b_i, c_lam, c_w_out):
    for layer in range(DEPTH):
        h = rmsnorm(x, g_mix_pre[layer])
        if layer % 2 == 0:
            e = layer // 2
            y = fox_shortconv_mixer(h, ab_w_in[e], ab_b_f[e], ab_conv_w[e], ab_w_out[e])
        else:
            o = layer // 2
            y = rglru_mixer(h, c_w_in[o], c_conv_w[o], c_conv_b[o], c_w_a[o], c_b_a[o],
                            c_w_i[o], c_b_i[o], c_lam[o], c_w_out[o])
        x = x + rmsnorm(y, g_mix_post[layer])
        h = rmsnorm(x, g_cross_pre[layer])
        m = rmsnorm(mem, g_mem[layer])
        y = memory_cross_attention(h, m, w_xq[layer], w_xkv[layer], w_xo[layer])
        x = x + rmsnorm(y, g_cross_post[layer])
        h = rmsnorm(x, g_ffn_pre[layer])
        y = swiglu(h, w_ffn_gu[layer], w_ffn_down[layer])
        x = x + rmsnorm(y, g_ffn_post[layer])
    return x


def setup_inputs(seed=0):
    out = dict(first_inputs(seed))
    for name, value in second_inputs(seed + 1).items():
        if name != "x":
            out[name + "_2"] = value
    return out


def reference(
    x, attn_norm, ffn_norm, final_norm, w_in_e, w_out_e, cmp_pe_k, cmp_pe_v, cmp_k_w1, cmp_k_w2,
    cmp_v_w1, cmp_v_w2, sinks, w_qkv_o, w_out_o, w_gate_up, w_down, mem_2, g_mix_pre_2,
    g_mix_post_2, g_cross_pre_2, g_mem_2, g_cross_post_2, g_ffn_pre_2, g_ffn_post_2, w_xq_2,
    w_xkv_2, w_xo_2, w_ffn_gu_2, w_ffn_down_2, ab_w_in_2, ab_b_f_2, ab_conv_w_2, ab_w_out_2,
    c_w_in_2, c_conv_w_2, c_conv_b_2, c_w_a_2, c_b_a_2, c_w_i_2, c_b_i_2, c_lam_2, c_w_out_2,
):
    x = first_block(
        x, attn_norm, ffn_norm, final_norm, w_in_e, w_out_e, cmp_pe_k, cmp_pe_v, cmp_k_w1,
        cmp_k_w2, cmp_v_w1, cmp_v_w2, sinks, w_qkv_o, w_out_o, w_gate_up, w_down,
    )
    return second_block(
        x, mem_2, g_mix_pre_2, g_mix_post_2, g_cross_pre_2, g_mem_2, g_cross_post_2,
        g_ffn_pre_2, g_ffn_post_2, w_xq_2, w_xkv_2, w_xo_2, w_ffn_gu_2, w_ffn_down_2, ab_w_in_2,
        ab_b_f_2, ab_conv_w_2, ab_w_out_2, c_w_in_2, c_conv_w_2, c_conv_b_2, c_w_a_2, c_b_a_2,
        c_w_i_2, c_b_i_2, c_lam_2, c_w_out_2,
    )


_drawn_inputs = setup_inputs


def setup_inputs(seed=0):
    import zlib

    import numpy as np

    out = dict(_drawn_inputs(seed))
    spreads = {}
    factors = {'attn_norm': 3.366,
     'cmp_pe_k': 8.0,
     'cmp_pe_v': 5.282,
     'sinks': 5.37,
     'g_mix_post_2': 2.758,
     'g_cross_pre_2': 3.58,
     'g_cross_post_2': 3.038,
     'g_ffn_pre_2': 2.822,
     'g_ffn_post_2': 4.235,
     'c_conv_b_2': 4.156,
     'c_b_a_2': 54.064,
     'c_b_i_2': 23.384}
    for name, (base, spread) in spreads.items():
        noise = np.random.default_rng([zlib.crc32(name.encode()), seed]).standard_normal(out[name].shape)
        drawn = base * np.exp(spread * noise) if base else spread * noise
        out[name] = __import__('jax').numpy.asarray(drawn.astype(out[name].dtype))
    for name, factor in factors.items():
        out[name] = (out[name] * factor).astype(out[name].dtype)
    return out
```

```python
from contextlib import ExitStack

import numpy as np

import concourse.bass as bass
from concourse import mybir

P = 128
D = 1024
KT = D // P
T = 512
TB = T // P
MEM = 256
MB = MEM // P
FF = 2816
FJ = FF // P
HD = 64
SCALE = HD ** -0.5
NC_CMP = T // 16 - 1
CT = 8
CW = CT * P
RING = 4
LEAD = RING - 1
DN_CHUNKS = 3
NEG = -1.0e30
ATANH_TERMS = 9
CONST_DMAS = 4
X_TOTAL = 7 * KT
PROJ_AB = 17 + 24

LINEARS = [
    ("in_e", 17, 1), ("cmp", 4, 2), ("out_e", 8, 1), ("gu0", 2 * FJ, 1), ("dn0", KT, DN_CHUNKS),
    ("qkv", 24, 1), ("out_o", 8, 1), ("gu1", 2 * FJ, 1), ("dn1", KT, DN_CHUNKS),
    ("ab_in", 25, 1), ("ab_out", 8, 1), ("xkv0", 16, 1), ("xq0", 8, 1), ("xo0", 8, 1),
    ("gu2", 2 * FJ, 1), ("dn2", KT, DN_CHUNKS),
    ("c_u", 8, 1), ("lru", 4, 1), ("c_gate", 8, 1), ("c_out", 8, 1), ("xkv1", 16, 1), ("xq1", 8, 1), ("xo1", 8, 1),
    ("gu3", 2 * FJ, 1), ("dn3", KT, DN_CHUNKS),
]
CHUNK0, BANK0 = {}, {}
_c = _g = 0
for _name, _m, _q in LINEARS:
    CHUNK0[_name], BANK0[_name] = _c, _g
    _c += _m * _q
    _g += 4 * _m if _name == "lru" else _m
N_CHUNKS = _c
TILES = {name: m for name, m, _ in LINEARS}

GAINS = ["attn0", "ffn0", "attn1", "ffn1", "final"] + [
    f"{n}{i}" for i in range(2)
    for n in ("mix_pre", "mix_post", "cross_pre", "mem", "cross_post", "ffn_pre", "ffn_post")]
SMALL, _at = {}, 0
for _name, _n in [(f"g_{n}", KT) for n in GAINS] + [
        ("sink", 8), ("pe", 32), ("w2v", 128), ("w2k", 256), ("abconv", 12), ("cconv", 32),
        ("cbias", 8), ("ba", 8), ("bi", 8), ("lam", 8), ("bf", 1)]:
    SMALL[_name] = slice(_at, _at + _n)
    _at += _n
N_SMALL = _at


class Seq:

    def __init__(self):
        self.n, self.i, self.per, self.base = 0, None, 0, 0

    def at(self, n):
        return n if self.i is None else self.i * self.per + (n - self.base)

    def next(self):
        self.n += 1
        return self.at(self.n)

    def enter(self, i, first, per):
        self.i, self.per, self.base, self.before = i, per, first * per, self.n

    def leave(self, times):
        assert self.n - self.before == self.per, (self.n - self.before, self.per)
        self.n = self.before + times * self.per
        self.i = None


def chunk_at(c, i, per):
    return c if i is None else i * per + c


def two_stacks(nc, x_in, mem_in, weights, small_in, tables_in, rope_in, cmpmask_in, sel_dram, out):
    f32, f32r = mybir.dt.float32, mybir.dt.float32r
    ALU, ACT, AX = mybir.AluOpType, mybir.ActivationFunctionType, mybir.AxisListType
    ctx = ExitStack()
    with ctx:
        def sb(name, shape, dt=f32):
            return ctx.enter_context(nc.sbuf_tensor(name, shape, dt))

        def sem(name):
            return ctx.enter_context(nc.semaphore(name))

        x = sb("x", [P, KT, T])
        w_raw = sb("w_raw", [P, RING, CW])
        w_hi = sb("w_hi", [P, RING, CW], f32r)
        w_lo = sb("w_lo", [P, RING, CW], f32r)
        xl = sb("xl", [P, KT, T], f32r)
        rope = sb("rope", [P, 2, T])
        rstd = sb("rstd", [P, T])
        acc = sb("acc", [P, T])
        tab = sb("tab", [P, T + 2 * P])
        ident = sb("ident", [P, P])
        ones = sb("ones", [P, P])
        tmpa = sb("tmpa", [P, 2, T])
        tmpb = sb("tmpb", [P, 2, T])
        small = sb("small", [P, N_SMALL])
        den = sb("den", [P, 4, 8])
        negm = sb("negm", [P, 4, 8])
        wgt = sb("wgt", [P, 8])
        c4 = sb("c4", [P, 8])
        c8 = sb("c8", [P, 8])
        lp = sb("lp", [P, 4, 8])
        negsink = sb("negsink", [P, 8])
        sinkarg = sb("sinkarg", [P, 2, 8])
        cst = sb("cst", [P, 2, 8])

        with nc.sbuf_tensor("xh", [P, KT, T], f32r) as xh:
            pass
        y_dn = sb("y_dn", [P, KT, T])

        def place(name, shape, kib, dt=f32):
            if kib == 0:
                with nc.sbuf_tensor(name, shape, dt) as here:
                    return here
            with nc.sbuf_tensor(name + "_below", [P, int(kib * 256)], f32):
                with nc.sbuf_tensor(name, shape, dt) as here:
                    return here

        hh = place("hh", [P, FJ, T], 0, f32r)
        hl = place("hl", [P, FJ, T], 44, f32r)
        z_c = place("z_c", [P, 2, T], 0)
        v_diag = place("v_diag", [P, 2, 4, HD], 0)
        pc_t = place("pc_t", [P, 2, P], 2)
        s_c = place("s_c", [P, 8, 32], 3)
        z_v0 = place("z_v0", [P, 3, T], 4)
        k_r0 = place("k_r0", [P, 3, T], 10)
        q_r0 = place("q_r0", [P, 8, T], 16)
        q_p0 = place("q_p0", [P, 4, T], 32)
        v_t0 = place("v_t0", [P, 3, TB, P], 40)
        gate_f = place("gate_f", [P, T], 46)
        gate_t = place("gate_t", [P, TB, 24], 48)
        cmask = place("cmask", [P, TB, 32], 48.5)
        hid = place("hid", [P, 2, 2, 62], 49)
        kc_t = place("kc_t", [P, 32], 50)
        mix0 = place("mix0", [P, TB, D], 51)
        blk = place("blk", [P, 16, 62], 67)
        blk_h = place("blk_h", [P, 2, 16, 62], 71, f32r)
        blk_l = place("blk_l", [P, 2, 16, 62], 79, f32r)
        rot0 = place("rot0", [P, 2, 2, T], 51)
        sm = place("sm", [P, 3, T], 69)
        pr = place("pr", [P, 3, T], 75)
        pt = place("pt", [P, 3, T], 81)
        q_r1 = place("q_r1", [P, 8, T], 0)
        k_r1 = place("k_r1", [P, 8, T], 16)
        v_t1 = place("v_t1", [P, 8, TB, P], 32)
        mix1 = place("mix1", [P, TB, D], 48)
        z_v1 = place("z_v1", [P, 8, T], 48)
        rot1 = place("rot1", [P, 2, 2, T], 69)
        q_f = place("q_f", [P, 4, T], 0)
        k_f = place("k_f", [P, 4, T], 8)
        z_vf = place("z_vf", [P, 4, T], 16)
        mix_f = place("mix_f", [P, TB, T], 16)
        v_tf = place("v_tf", [P, 4, TB, P], 24)
        gated = place("gated", [P, 4, 2 + T], 32)
        conv_f = place("conv_f", [P, 4, T], 41)
        cum = place("cum", [8, T], 57)
        cum_h = place("cum_h", [8, T], 49, f32r)
        cum_l = place("cum_l", [8, T], 51, f32r)
        sel_r = place("sel_r", [8, 8, P], 53, f32r)
        fw = place("fw", [8, 4, T], 59)
        sel = place("sel", [8, 8, P], 59)
        q_x = place("q_x", [P, 8, T], 0)
        k_x = place("k_x", [P, 8, MEM], 16)
        v_x = place("v_x", [P, MB, D], 24)
        mem_h = place("mem_h", [P, KT, MEM], 32, f32r)
        mem_l = place("mem_l", [P, KT, MEM], 40, f32r)
        y_mid = place("y_mid", [P, KT, T], 48)
        mix_x = place("mix_x", [P, TB, D], 48)
        mem = place("mem", [P, KT, MEM], 64)
        z_vx = place("z_vx", [P, 8, MEM], 72)
        rstd_m = place("rstd_m", [P, MEM], 87)
        i_l = place("i_l", [P, 8, T], 0)
        gate_r = place("gate_r", [P, 8, T], 0)
        y_l = place("y_l", [P, 8, T], 0, f32r)
        u_r = place("u_r", [P, 8, T], 16)
        y_h = place("y_h", [P, 8, T], 16, f32r)
        r_l = place("r_l", [P, 8, T], 32)
        u_h = place("u_h", [P, 8, T], 48, f32r)
        decay = place("decay", [P, 8, T], 48)
        u_l = place("u_l", [P, 8, T], 64, f32r)
        z_u = place("z_u", [P, 2, 3 + T], 80)

        ps = ctx.enter_context(nc.psum_tensor("ps", [P, 8, T], f32))
        S_BANKS, PT_BANKS, O_BANKS, MISC = (0, 1, 2), (3, 6), (4, 5), 7

        w_in = [sem(f"w_in{s}") for s in range(RING)]
        hi_ready = sem("hi_ready")
        lo_ready = sem("lo_ready")
        chunk_done = sem("chunk_done")
        evac_done = sem("evac_done")
        const_in, small_in_sem = sem("const_in"), sem("small_in_sem")
        x_in_sem = [sem(f"x_in{j}") for j in range(KT // 2)]
        tab_in = sem("tab_in")
        mem_in_sem = sem("mem_in_sem")
        out_done = sem("out_done")
        pool_set = sem("pool_set")
        dve_self = sem("dve_self")
        act_self = sem("act_self")
        x_ready = sem("x_ready")
        xh_ready = sem("xh_ready")
        xl_ready = sem("xl_ready")
        acc_ready = sem("acc_ready")
        ss_done = sem("ss_done")
        var_done = sem("var_done")
        sd_done = sem("sd_done")
        silu_ready, prod_ready = sem("silu_ready"), sem("prod_ready")
        hh_ready, hl_ready = sem("hh_ready"), sem("hl_ready")
        swap_ready = sem("swap_ready")
        proj_ready = sem("proj_ready")
        s_ready, sm_done, p_ready = sem("s_ready"), sem("sm_done"), sem("p_ready")
        pt_ready = sem("pt_ready")
        pt_copied = [sem("pt_copied_dve"), sem("pt_copied_act")]
        o_done, o_free = sem("o_done"), sem("o_free")
        sink_in, sink_out = sem("sink_in"), sem("sink_out")
        vt_ready, vt_copied = sem("vt_ready"), sem("vt_copied")
        mt_ready, mixh_ready, mixl_ready = sem("mt_ready"), sem("mixh_ready"), sem("mixl_ready")
        act_in, act_out = sem("act_in"), sem("act_out")
        cmp_ps, cmp_sb = sem("cmp_ps"), sem("cmp_sb")
        cmp_half = sem("cmp_half")
        cmp_vk = sem("cmp_vk")
        blk_copied, blk_added = sem("blk_copied"), sem("blk_added")
        blk_hi, cmp_blk = sem("blk_hi"), sem("cmp_blk")
        cmp_hid = sem("cmp_hid")
        cmp_masked = sem("cmp_masked")
        gate_sig = sem("gate_sig")
        feat_in, feat_hi, feat_ready = sem("feat_in"), sem("feat_hi"), sem("feat_ready")
        mem_ready, mem_hi = sem("mem_ready"), sem("mem_hi")
        sel_in, sel_ready, cum_ready = sem("sel_in"), sem("sel_ready"), sem("cum_ready")
        STATES = {3: (0, 1), 4: (2, 3), 5: (4, 5), 6: (6,), 7: (7,)}
        u_conv, u_hi = sem("u_conv"), sem("u_hi")
        gelu_done, lru_act = sem("gelu_done"), sem("lru_act")

        def gain(name, m):
            s = SMALL[f"g_{name}"].start + m
            return small[:, s:s + 1]

        def col(name, a, b=None):
            s = SMALL[name].start
            return small[:, s + a:s + (a + 1 if b is None else b)]

        def heads_of(tile, pair):
            return (tile, tile + 4) if pair == "grouped" else (2 * tile, 2 * tile + 1)

        def unit(qk, nk, mask, scale, values, o_cols, index, last, sink=None):
            return dict(qk=qk, nk=nk, mask=mask, scale=scale, values=values, o=o_cols,
                        index=index, last=last, sink=sink)

        def tokens(t):
            return slice(t * P, (t + 1) * P)

        def units_layer0():
            out_units = []
            for t in range(TB):
                for branch in ("B", "sel", "win"):
                    first = max(0, t - 1) if branch == "B" else 0
                    nk = (t + 1 - first) * P
                    which = {"sel": 0, "win": 1, "B": 2}[branch]
                    mask = tab[:, T + 2 * P - nk:T + 2 * P] if branch == "B" else tab[:, T - nk:T]
                    for h in (0, 4, 1, 5, 2, 6, 3, 7):
                        j, b = h % 4, h // 4
                        rows = slice(b * HD, (b + 1) * HD)
                        q = q_r0[rows, j + (4 if branch == "B" else 0), tokens(t)]
                        k = k_r0[rows, which, first * P:(t + 1) * P]
                        vals = [v_t0[:, which, kb, rows] for kb in range(first, t + 1)]
                        last = ("mix", branch, t, 0) if h == 7 else None
                        out_units.append(unit([(q, k)], nk, mask, SCALE, vals,
                                              (h * HD, HD), h, last, h if branch == "B" else None))
            return out_units

        def units_causal(q, k, v, tiles, groups_of, scale, forget=False):
            out_units = []
            for t in range(TB):
                for h in range(2 * tiles):
                    j, b = h // 2, h % 2
                    rows = slice(b * HD, (b + 1) * HD)
                    qk = [(q[rows, j, tokens(t)], k[rows, j, 0:(t + 1) * P])]
                    if forget:
                        qk += [(sel_r[0:8, h, :], c[0:8, 0:(t + 1) * P]) for c in (cum_h, cum_l)]
                    vals = [v[:, j, kb, rows] for kb in range(t + 1)]
                    g = h % 8
                    last = (("mix", "plain", t, h // 8)) if g == 7 else None
                    out_units.append(unit(qk, (t + 1) * P, tab[:, T - (t + 1) * P:T], scale, vals,
                                          (g * HD, HD), g, last))
            return out_units

        def units_memory():
            out_units = []
            for t in range(TB):
                for h in range(4):
                    qk = [(q_x[:, 2 * h + a, tokens(t)], k_x[:, 2 * h + a, :]) for a in range(2)]
                    vals = [v_x[:, kb, h * 256:(h + 1) * 256] for kb in range(MB)]
                    last = ("mix", "memory", t, h // 2) if h % 2 else None
                    out_units.append(unit(qk, MEM, tab[:, 0:MEM], 1 / 16, vals,
                                          (h % 2 * 256, 256), h % 2, last))
            return out_units

        U0, U1 = units_layer0(), units_causal(q_r1, k_r1, v_t1, 8, 2, SCALE)
        UF, UX = units_causal(q_f, k_f, v_tf, 4, 1, SCALE, forget=True), units_memory()
        LAG = 2

        block = ctx.enter_context(nc.Block())

        @block.sync
        def _(sp):
            def load(c, slot, i=None):
                sp.dma_start(w_raw[:, slot, :],
                             weights[c] if i is None else
                             weights[bass.ds(c, 1)].rearrange("a p n -> p (a n)")).then_inc(w_in[slot], 16)

            for c in range(RING):
                load(c, c)
            with sp.Fori(1, N_CHUNKS // RING) as i:
                for u in range(RING):
                    sp.wait_ge(lo_ready, i * RING + (u + 1 - RING))
                    load(i * RING + u, u, i)
            for c in range(N_CHUNKS // RING * RING, N_CHUNKS):
                sp.wait_ge(lo_ready, c + 1 - RING)
                load(c, c % RING)
            for m in range(0, KT, 2):
                sp.wait_ge(x_ready, X_TOTAL - KT + m + 2)
                sp.dma_start(out[:, m:m + 2], x[:, m:m + 2]).then_inc(out_done, 16)
            sp.wait_ge(out_done, KT // 2 * 16)

        @block.gpsimd
        def _(pool):
            nc.gpsimd.memset(ones[:], 1.0).then_inc(pool_set, 1)

            def low(slot):
                nc.gpsimd.tensor_tensor(w_lo[:, slot], w_raw[:, slot], w_hi.bitcast(f32)[:, slot],
                                        ALU.subtract).then_inc(lo_ready, 1)

            for c in range(RING):
                pool.wait_ge(hi_ready, c + 1)
                low(c)
            with pool.Fori(1, N_CHUNKS // RING) as i:
                for u in range(RING):
                    pool.wait_ge(hi_ready, i * RING + (u + 1))
                    pool.wait_ge(chunk_done, i * RING + (u + 1 - RING))
                    low(u)
            for c in range(N_CHUNKS // RING * RING, N_CHUNKS):
                pool.wait_ge(hi_ready, c + 1)
                pool.wait_ge(chunk_done, c + 1 - RING)
                low(c % RING)

        @block.tensor
        def _(pe):
            xl_s, mixl, hl_s = Seq(), Seq(), Seq()
            accs, vts, units_seen, groups = Seq(), Seq(), Seq(), Seq()
            mts, projs = Seq(), Seq()

            def product(dst, slot, tile, hi, lo, first, last):
                w = slice(tile * P, (tile + 1) * P)
                nc.tensor.matmul(dst, w_hi[:, slot, w], hi, start=first, stop=False)
                nc.tensor.matmul(dst, w_hi[:, slot, w], lo, start=False, stop=False)
                return nc.tensor.matmul(dst, w_lo[:, slot, w], hi, start=False, stop=last)

            def linear(name, n_k, rhs, n=T, ready=None, after_first=None, looped=True):
                c0, g0, tiles = CHUNK0[name], BANK0[name], TILES[name]
                per_tile = -(-n_k // CT)

                def out_tile(m, i):
                    g = g0 + m
                    if i is not None:
                        pe.wait_ge(evac_done, i * RING + (g - 3))
                    elif g >= 4:
                        pe.wait_ge(evac_done, g - 3)
                    for k in range(n_k):
                        c = c0 + m * per_tile + k // CT
                        if k % CT == 0:
                            pe.wait_ge(lo_ready, chunk_at(c + 1, i, RING * per_tile))
                        if m == 0 and ready is not None and (i is None or after_first is None):
                            ready(k)
                        hi, lo = rhs(m, k)
                        last = product(ps[:, g % 4, 0:n], c % RING, k % CT, hi, lo, k == 0, k == n_k - 1)
                        if k % CT == CT - 1 or k == n_k - 1:
                            last.then_inc(chunk_done, 1)

                whole = tiles // RING
                first = 0
                if after_first is not None or not looped:
                    for m in range(RING if looped else tiles):
                        out_tile(m, None)
                        if m == 0 and after_first is not None:
                            after_first()
                    if not looped:
                        return
                    first = 1
                if whole - first == 1:
                    for m in range(first * RING, whole * RING):
                        out_tile(m, None)
                elif whole > first:
                    with pe.Fori(first, whole) as i:
                        for m in range(RING):
                            out_tile(m, i)
                for m in range(whole * RING, tiles):
                    out_tile(m, None)

            def x_tiles(m, k):
                return xh[:, k, :], xl[:, k, :]

            def x_tile_ready(k):
                pe.wait_ge(xl_ready, xl_s.next())

            def mix_tile_ready(n):
                def ready(k):
                    if k == 0:
                        pe.wait_ge(mixl_ready, n)
                return ready

            def sum_squares(n=T):
                accs.n += KT - 1
                pe.wait_ge(vt_copied, vts.n)
                pe.wait_ge(acc_ready, accs.n)
                nc.tensor.matmul(ps[:, MISC, 0:n], ones[:], acc[:, 0:n], start=True,
                                 stop=True).then_inc(ss_done, 1)

            def transpose_values(z, tiles):
                for j in range(tiles):
                    n = vts.next()
                    if n > 4:
                        pe.wait_ge(vt_copied, n - 4)
                    bank = 4 + (n - 1) % 4
                    for kb in range(TB):
                        last = nc.tensor.transpose(ps[:, bank, tokens(kb)], z[:, j, tokens(kb)], ident[:])
                    last.then_inc(vt_ready, 1)

            def attention(units, hooks):
                u0 = units_seen.n
                units_seen.n += len(units)
                pairs = len(units) // 2
                for s in range(pairs + 2):
                    if s < pairs:
                        two = [(units[2 * s + a], u0 + 2 * s + a) for a in range(2)]
                        for u, n in two:
                            if n >= 3:
                                pe.wait_ge(sm_done, n - 2)
                        parts = len(two[0][0]["qk"])
                        for a in range(parts):
                            for u, n in two:
                                q, k = u["qk"][a]
                                last = nc.tensor.matmul(ps[:, S_BANKS[n % 3], 0:u["nk"]], q, k,
                                                        start=a == 0, stop=a == parts - 1)
                                if a == parts - 1:
                                    last.then_inc(s_ready, 1)
                    if s >= 2:
                        for n in (u0 + 2 * s - 4, u0 + 2 * s - 3):
                            u = units[n - u0]
                            if u["index"] == 0:
                                g = groups.next() - 1
                                if g >= 2:
                                    pe.wait_ge(o_free, g - 1)
                            pe.wait_ge(pt_copied[n % 2], n // 2 + 1)
                            a, w = u["o"]
                            dst = ps[:, O_BANKS[(groups.n - 1) % 2], a:a + w]
                            for kb, v in enumerate(u["values"]):
                                last = nc.tensor.matmul(dst, pt[:, n % 3, tokens(kb)], v, start=kb == 0,
                                                        stop=kb == len(u["values"]) - 1)
                            last.then_inc(o_done, 1)
                    if 1 <= s <= pairs:
                        for n in (u0 + 2 * s - 2, u0 + 2 * s - 1):
                            pe.wait_ge(p_ready, n + 1)
                            if n >= 2:
                                pe.wait_ge(pt_copied[n % 2], n // 2)
                            for kb in range(units[n - u0]["nk"] // P):
                                last = nc.tensor.transpose(ps[:, PT_BANKS[n % 2], tokens(kb)],
                                                           pr[:, n % 3, tokens(kb)], ident[:])
                            last.then_inc(pt_ready, 1)
                    for hook in hooks.get(s, []):
                        hook()

            def transpose_mix(mix, t, blocks=8, begun=0):
                pe.wait_ge(o_free, groups.n - begun)
                for half in range(blocks // 4):
                    if mts.n:
                        pe.wait_ge(mixl_ready, mts.n)
                    for q in range(4):
                        last = nc.tensor.transpose(ps[:, MISC, tokens(q)],
                                                   mix[:, t, tokens(half * 4 + q)], ident[:])
                    last.then_inc(mt_ready, 1)
                    mts.next()

            def mix_hooks(units, mix, blocks=8, begun=1):
                per = len(units) // TB // 2
                return {t * per + LAG: [lambda t=t: transpose_mix(mix, t - 1, blocks, begun)]
                        for t in range(1, TB)}

            pe.wait_ge(const_in, CONST_DMAS * 16)
            pe.wait_ge(pool_set, 1)

            linear("in_e", KT, x_tiles, ready=x_tile_ready, after_first=sum_squares)
            projs.n += 17
            pe.wait_ge(proj_ready, projs.n)
            transpose_values(z_v0, 3)
            pe.wait_ge(gate_sig, 1)
            for t in range(TB):
                last = nc.tensor.transpose(ps[:, 3, t * 32:t * 32 + 24], gate_f[0:24, tokens(t)],
                                           ident[0:24, 0:24])
            last.then_inc(cmp_ps, 1)
            pe.wait_ge(cmp_blk, 2)
            pe.wait_ge(cmp_sb, 1)
            linear("cmp", 16, lambda m, k: (blk_h[:, m // 2, k, :], blk_l[:, m // 2, k, :]),
                   n=62, looped=False)
            pe.wait_ge(cmp_sb, 2)
            pe.wait_ge(vt_copied, vts.n)
            for j in range(2):
                nc.tensor.matmul(ps[:, MISC, 0:62], col("w2k", j * P, (j + 1) * P), hid[:, 0, j, :],
                                 start=j == 0, stop=j == 1)
            for g in range(2):
                for j in range(2):
                    last = nc.tensor.matmul(ps[0:31, MISC, 128 + g * HD:128 + (g + 1) * HD],
                                            hid[:, 1, j, g * 31:(g + 1) * 31],
                                            col("w2v", j * HD, (j + 1) * HD), start=j == 0, stop=j == 1)
            last.then_inc(cmp_ps, 1)
            pe.wait_ge(cmp_vk, 1)

            def cmp_scores(t):
                def run():
                    if mts.n:
                        pe.wait_ge(mixl_ready, mts.n)
                    if t:
                        pe.wait_ge(cmp_sb, 2 + 2 * t)
                    for h in range(8):
                        j, b = h % 4, h // 4
                        rows = slice(b * HD, (b + 1) * HD)
                        if h == 4:
                            pe.wait_ge(cmp_half, t + 1)
                        last = nc.tensor.matmul(ps[:, MISC, h * 32:(h + 1) * 32],
                                                q_p0[rows, j, tokens(t)], kc_t[rows, :],
                                                start=True, stop=True)
                        if h == 3:
                            last.then_inc(cmp_half, 1)
                    last.then_inc(cmp_ps, 1)
                return run

            def cmp_transposes(t):
                def run():
                    pe.wait_ge(cmp_sb, 3 + 2 * t)
                    for g in range(2):
                        last = nc.tensor.transpose(
                            ps[:, MISC, 256 + g * P:256 + (g + 1) * P],
                            s_c[:, 4 * g:4 * g + 4, :].rearrange("p h c -> p (h c)"), ident[:])
                    last.then_inc(cmp_ps, 1)
                return run

            def cmp_values(t):
                def run():
                    g_no = groups.next() - 1
                    if g_no >= 2:
                        pe.wait_ge(o_free, g_no - 1)
                    pe.wait_ge(cmp_sb, 4 + 2 * t)
                    for g in range(2):
                        last = nc.tensor.matmul(ps[:, O_BANKS[g_no % 2], g * 256:(g + 1) * 256],
                                                pc_t[:, g, :],
                                                v_diag[:, g].rearrange("p h d -> p (h d)"),
                                                start=True, stop=True)
                    last.then_inc(cmp_ps, 1)
                return run

            hooks = mix_hooks(U0, mix0, begun=2)
            for t in range(1, TB):
                hooks.setdefault(12 * t - 2, []).append(cmp_scores(t))
                hooks.setdefault(12 * t, []).append(cmp_transposes(t))
                hooks.setdefault(12 * t + 1, []).append(cmp_values(t))
            cmp_scores(0)()
            cmp_transposes(0)()
            hooks.setdefault(1, []).append(cmp_values(0))
            attention(U0, hooks)
            transpose_mix(mix0, TB - 1)

            def feed_forward(f):
                linear(f"gu{f}", KT, x_tiles, ready=x_tile_ready, after_first=sum_squares)
                hl_s.n += FJ

                def hidden_ready(k):
                    pe.wait_ge(hl_ready, hl_s.n - FJ + k + 1)
                linear(f"dn{f}", FJ, lambda m, k: (hh[:, k, :], hl[:, k, :]), ready=hidden_ready)

            linear("out_e", KT, x_tiles, ready=mix_tile_ready(mts.n))
            feed_forward(0)

            linear("qkv", KT, x_tiles, ready=x_tile_ready, after_first=sum_squares)
            projs.n += 24
            pe.wait_ge(proj_ready, projs.n - 16)
            transpose_values(z_v1, 8)
            pe.wait_ge(proj_ready, projs.n)
            pe.wait_ge(vt_copied, vts.n)
            attention(U1, mix_hooks(U1, mix1, begun=1))
            transpose_mix(mix1, TB - 1)
            linear("out_o", KT, x_tiles, ready=mix_tile_ready(mts.n))
            feed_forward(1)
            sum_squares()

            def memory_attention(e):
                def kv_ready(k):
                    if k == 0:
                        pe.wait_ge(mem_ready, (e + 1) * KT)
                linear(f"xkv{e}", KT, lambda m, k: (mem_h[:, k, :], mem_l[:, k, :]), n=MEM,
                       ready=kv_ready, after_first=sum_squares)
                projs.n += 16
                pe.wait_ge(proj_ready, projs.n)
                for j in range(4):
                    n = vts.next()
                    pe.wait_ge(vt_copied, n - 4)
                    bank = 4 + (n - 1) % 4
                    for a in range(2):
                        for kb in range(MB):
                            last = nc.tensor.transpose(
                                ps[:, bank, kb * 256 + a * P:kb * 256 + (a + 1) * P],
                                z_vx[:, 2 * j + a, tokens(kb)], ident[:])
                    last.then_inc(vt_ready, 1)
                linear(f"xq{e}", KT, x_tiles, ready=x_tile_ready, after_first=sum_squares)
                projs.n += 8
                pe.wait_ge(proj_ready, projs.n)
                pe.wait_ge(vt_copied, vts.n)
                attention(UX, mix_hooks(UX, mix_x, begun=1))
                transpose_mix(mix_x, TB - 1)
                linear(f"xo{e}", KT, x_tiles, ready=mix_tile_ready(mts.n))
                sum_squares()
                linear(f"gu{2 + e}", KT, x_tiles, ready=x_tile_ready, after_first=sum_squares)
                hl_s.n += FJ

                def hidden_ready(k):
                    pe.wait_ge(hl_ready, hl_s.n - FJ + k + 1)
                linear(f"dn{2 + e}", FJ, lambda m, k: (hh[:, k, :], hl[:, k, :]), ready=hidden_ready)
                sum_squares()

            linear("ab_in", KT, x_tiles, ready=x_tile_ready, after_first=sum_squares)
            projs.n += 25
            pe.wait_ge(proj_ready, projs.n - 20)
            transpose_values(z_vf, 4)
            pe.wait_ge(proj_ready, projs.n)
            pe.wait_ge(vt_copied, vts.n)
            pe.wait_ge(sel_ready, 1)
            pe.wait_ge(cum_ready, 1)
            attention(UF, mix_hooks(UF, mix_f, blocks=4, begun=1))
            transpose_mix(mix_f, TB - 1, 4)

            def ab_ready(k):
                if k == 0:
                    pe.wait_ge(mixl_ready, mts.n)
                if k >= 4:
                    pe.wait_ge(feat_ready, k - 3)
            linear("ab_out", KT, x_tiles, ready=ab_ready,
                   after_first=lambda: sum_squares(MEM))
            memory_attention(0)

            linear("c_u", KT, x_tiles, ready=x_tile_ready, after_first=sum_squares)
            for n in range(4):
                pe.wait_ge(proj_ready, projs.n + 2 * n + 2)
                c = CHUNK0["lru"] + n
                pe.wait_ge(lo_ready, c + 1)
                for m in range(4):
                    g = BANK0["lru"] + 4 * n + m
                    pe.wait_ge(evac_done, g - 3)
                    for k in range(2):
                        last = product(ps[:, g % 4, :], c % RING, 2 * m + k, u_h[:, 2 * n + k, :],
                                       u_l[:, 2 * n + k, :], k == 0, k == 1)
                last.then_inc(chunk_done, 1)
            projs.n += 8
            linear("c_gate", KT, x_tiles)
            linear("c_out", KT, lambda m, k: (y_h[:, k, :], y_l[:, k, :]),
                   ready=lambda k: pe.wait_ge(feat_ready, 4 + k + 1),
                   after_first=lambda: sum_squares(MEM))
            memory_attention(1)

        class Shared:

            def __init__(self):
                self.x = Seq()
                self.xh = Seq()
                self.var = Seq()
                self.sd = Seq()
                self.silu = Seq()
                self.prod = Seq()
                self.hh = Seq()
                self.swap = Seq()
                self.units = Seq()
                self.unit_groups = Seq()
                self.vt = Seq()
                self.mt = Seq()
                self.mixh = Seq()
                self.act_in = Seq()
                self.act_out = Seq()
                self.sink = Seq()
                self.acc = Seq()
                self.ss = Seq()
                self.dself = Seq()
                self.memh = Seq()

        @block.scalar
        def _(act):
            n_ = Shared()
            A = nc.scalar.activation

            act.dma_start(small[:], small_in).then_inc(small_in_sem, 16)
            for m in range(0, KT, 2):
                act.dma_start(x[:, m:m + 2], x_in[:, m:m + 2]).then_inc(x_in_sem[m // 2], 16)
            act.dma_start(ident[:], tables_in[:, 0:P]).then_inc(const_in, 16)
            act.dma_start(rope[:], rope_in).then_inc(const_in, 16)
            act.dma_start(tab[:], tables_in[:, P:P + T + 2 * P]).then_inc(const_in, 16)
            act.dma_start(cmask[:], cmpmask_in).then_inc(const_in, 16)

            def high(c, i=None, per=0):
                if i is None and c >= N_CHUNKS:
                    return
                s = c % RING
                act.wait_ge(w_in[s], chunk_at(16 * (c // RING + 1), i, 16 * per // RING))
                if c >= RING or i is not None:
                    act.wait_ge(chunk_done, chunk_at(c + 1 - RING, i, per))
                A(w_hi[:, s], w_raw[:, s], ACT.Copy).then_inc(hi_ready, 1)

            def square(src, m, n=T):
                if m >= 3:
                    act.wait_ge(acc_ready, n_.acc.n + m - 2)
                if m == KT - 1:
                    n_.acc.n += KT - 1
                return A(acc[:, 0:n] if m == 0 else tmpa[:, m % 2, 0:n], src, ACT.Square)

            def publish(m, name):
                square(x[:, m], m)
                A(xh[:, m], x[:, m], ACT.Copy, scale=gain(name, m)).then_inc(xh_ready, 1)

            def publish_square(src, m):
                square(src, m).then_inc(xh_ready, 1)

            def root(n=T):
                act.wait_ge(var_done, n_.var.next())
                A(tmpb[:, 0, 0:n], tmpb[:, 0, 0:n], ACT.Sqrt).then_inc(sd_done, 1)

            def steps(name):
                c0 = CHUNK0[name]
                for m in range(TILES[name]):
                    high(c0 + m + LEAD)
                    yield m, BANK0[name] + m

            def swap_halves(dst, src, g):
                act.wait_ge(evac_done, g + 1)
                for a in (0, 64):
                    A(dst[a:a + 32], src[a + 32:a + 64], ACT.Copy)
                    last = A(dst[a + 32:a + 64], src[a:a + 32], ACT.Copy)
                last.then_inc(swap_ready, 1)

            def copy_values(dst, n):
                act.wait_ge(vt_ready, n_.vt.next())
                bank = ps[:, 4 + (n_.vt.n - 1) % 4, :]
                A(dst, bank.rearrange("p (k c) -> p k c", c=dst.shape[-1]), ACT.Copy).then_inc(vt_copied, 1)

            def attention(units, hooks):
                u0 = n_.units.n
                n_.units.n += len(units)
                pairs = len(units) // 2
                for s in range(pairs + 2):
                    for a in range(2 * s, 2 * s + 2 if s < pairs else 0):
                        u, n = units[a], u0 + a
                        slot, h = n_.unit_groups.n % 4, u["index"]
                        act.wait_ge(sm_done, n + 1)
                        if n >= 3:
                            act.wait_ge(pt_ready, n - 2)
                        A(pr[:, n % 3, 0:u["nk"]], sm[:, n % 3, 0:u["nk"]], ACT.Exp, scale=-1.0,
                          bias=negm[:, slot, h:h + 1],
                          accum_out=den[:, slot, h:h + 1]).then_inc(p_ready, 1)
                        if u["last"]:
                            if u["sink"] is not None:
                                act.wait_ge(sink_in, n_.sink.next())
                                A(sinkarg[:, 1], sinkarg[:, 0], ACT.Exp).then_inc(sink_out, 1)
                            n_.unit_groups.next()
                    if 1 <= s <= pairs:
                        n = u0 + 2 * s - 1
                        nk = units[n - u0]["nk"]
                        act.wait_ge(pt_ready, n + 1)
                        if n >= 3:
                            act.wait_ge(o_done, n - 2)
                        A(pt[:, n % 3, 0:nk], ps[:, PT_BANKS[n % 2], 0:nk],
                          ACT.Copy).then_inc(pt_copied[1], 1)
                    for hook in hooks.get(s, []):
                        hook()

            def split_mix(t, blocks=8):
                for half in range(blocks // 4):
                    act.wait_ge(mt_ready, n_.mt.next())
                    A(xh[:, 4 * half:4 * half + 4, tokens(t)],
                      ps[:, MISC, :].rearrange("p (f q) -> p f q", f=4), ACT.Copy).then_inc(mixh_ready, 1)

            def mix_hooks(units, blocks=8):
                per = len(units) // TB // 2
                return {t * per + LAG: [lambda t=t: split_mix(t - 1, blocks)] for t in range(1, TB)}

            def exp_neg_abs(dst, src):
                act.wait_ge(act_in, n_.act_in.next())
                A(dst, src, ACT.Exp, scale=-1.0).then_inc(act_out, 1)

            def gate_up(f):
                name = f"gu{f}"
                c0, g0 = CHUNK0[name], BANK0[name]

                def pair(j, i):
                    high(c0 + 2 * j + LEAD, i, 4)
                    high(c0 + 2 * j + 1 + LEAD, i, 4)
                    if i is None and j == 0:
                        root()
                    act.wait_ge(evac_done, chunk_at(g0 + 2 * j + 2, i, 4))
                    A(tmpa[:, j % 2], tmpa[:, j % 2], ACT.Silu).then_inc(silu_ready, 1)
                    act.wait_ge(prod_ready, n_.prod.next())
                    dst = hh[:, j, :] if i is None else \
                        hh[:, bass.ds(i * 2 + j, 1), :].rearrange("p a t -> p (a t)")
                    A(dst, tmpb[:, j % 2], ACT.Copy).then_inc(hh_ready, 1)

                pair(0, None)
                pair(1, None)
                with act.Fori(1, FJ // 2) as i:
                    n_.prod.enter(i, 1, 2)
                    pair(0, i)
                    pair(1, i)
                n_.prod.leave(FJ // 2 - 1)

            def down(f, after):
                for m in range(KT):
                    for q in range(DN_CHUNKS):
                        high(CHUNK0[f"dn{f}"] + DN_CHUNKS * m + q + LEAD)
                    act.wait_ge(evac_done, BANK0[f"dn{f}"] + m + 1)
                    after(m)

            act.wait_ge(small_in_sem, 16)
            exp_neg_abs(lp[:, 1], lp[:, 0])
            for m in range(KT):
                act.wait_ge(x_in_sem[m // 2], 16)
                publish(m, "attn0")
                if m < LEAD:
                    high(m)
            act.wait_ge(const_in, CONST_DMAS * 16)
            for m, g in steps("in_e"):
                if m == 0:
                    root()
                if m in (1, 3):
                    kv = m // 2
                    act.wait_ge(evac_done, kv + 1)
                    if kv:
                        act.wait_ge(cmp_blk, 1)
                    for h in range(2):
                        zv = z_c[h * HD:(h + 1) * HD, kv].rearrange("p (c r s) -> p r c s", r=8, s=2)
                        for s in range(2):
                            dst = blk[s * HD:(s + 1) * HD]
                            A(dst[:, 0:8, h * 31:(h + 1) * 31], zv[:, :, 0:31, s], ACT.Copy)
                            last = A(dst[:, 8:16, h * 31:(h + 1) * 31], zv[:, :, 1:32, s], ACT.Copy)
                    last.then_inc(blk_copied, 1)
                if m in (2, 4):
                    act.wait_ge(blk_added, m // 2)
                    A(blk_h[:, m // 2 - 1], blk[:], ACT.Copy).then_inc(blk_hi, 1)
                if 5 <= m < 16:
                    src = q_p0[:, m - 8] if 8 <= m < 12 else rot0[:, m % 2, 0]
                    swap_halves(rot0[:, m % 2, 1], src, g)
                if m == 16:
                    act.wait_ge(evac_done, g + 1)
                    A(gate_f[0:24], gate_f[0:24], ACT.Sigmoid).then_inc(gate_sig, 1)
            for j in range(3):
                copy_values(v_t0[:, j], j)
            act.wait_ge(cmp_ps, 1)
            A(gate_t[:], ps[:, 3, 0:128].rearrange("p (t c) -> p t c", t=TB)[:, :, 0:24],
              ACT.Copy).then_inc(cmp_sb, 1)
            for q in range(8):
                high(CHUNK0["cmp"] + q + LEAD)
                if q % 2:
                    act.wait_ge(cmp_hid, q // 2 + 1)
                    last = A(hid[:, q // 4, q // 2 % 2], hid[:, q // 4, q // 2 % 2], ACT.Silu)
            last.then_inc(cmp_sb, 1)

            def cmp_exp(t):
                act.wait_ge(cmp_masked, t + 1)
                A(s_c[:], s_c[:], ACT.Exp, scale=SCALE).then_inc(cmp_sb, 1)

            def cmp_copy(t):
                act.wait_ge(cmp_ps, 4 + 3 * t)
                A(pc_t[:], ps[:, MISC, 256:512].rearrange("p (g q) -> p g q", g=2),
                  ACT.Copy).then_inc(cmp_sb, 1)

            hooks = mix_hooks(U0)
            for t in range(1, TB):
                hooks.setdefault(12 * t - 2, []).append(lambda t=t: cmp_exp(t))
                hooks.setdefault(12 * t, []).append(lambda t=t: cmp_copy(t))
            cmp_exp(0)
            cmp_copy(0)
            attention(U0, hooks)
            split_mix(TB - 1)

            def residual_out(name, gname):
                for m, g in steps(name):
                    pass
                act.wait_ge(evac_done, BANK0[name] + KT)
                for m in range(KT):
                    publish(m, gname)

            residual_out("out_e", "ffn0")
            gate_up(0)
            down(0, lambda m: publish(m, "attn1"))

            for m, g in steps("qkv"):
                if m == 0:
                    root()
                if m == 8:
                    act.dma_start(tab[:, 0:T], tables_in[:, P + T + 2 * P:2 * P + 2 * T + P]).then_inc(tab_in, 16)
                if m >= 8:
                    swap_halves(rot1[:, m % 2, 1], rot1[:, m % 2, 0], g)
            for j in range(8):
                copy_values(v_t1[:, j], j)
            attention(U1, mix_hooks(U1))
            split_mix(TB - 1)
            act.dma_start(tab[:, 0:T], tables_in[:, P:P + T]).then_inc(tab_in, 16)
            residual_out("out_o", "ffn1")
            gate_up(1)
            down(1, lambda m: publish_square(x[:, m], m))
            root()

            def renormed(m, name):
                act.wait_ge(x_ready, n_.x.next())
                publish(m, name)

            for m in range(KT):
                renormed(m, "mix_pre0")

            def load_memory():
                act.dma_start(mem[:], mem_in).then_inc(mem_in_sem, 16)

            def publish_memory(e):
                act.wait_ge(mem_in_sem, 16 * (e + 1))
                for m in range(KT):
                    square(mem[:, m], m, MEM)
                    A(mem_h[:, m], mem[:, m], ACT.Copy, scale=gain(f"mem{e}", m)).then_inc(mem_hi, 1)

            def normed_out(name):
                for m, g in steps(name):
                    if m == 0 and name in ("ab_out", "c_out"):
                        root(MEM)
                    act.wait_ge(evac_done, g + 1)
                    publish_square(y_mid[:, m], m)

            def memory_attention(e):
                for m, g in steps(f"xkv{e}"):
                    if m == 0:
                        root()
                    if m < KT:
                        renormed(m, f"cross_pre{e}")
                for j in range(4):
                    copy_values(v_x[:, :, j * 256:(j + 1) * 256], j)
                for m, g in steps(f"xq{e}"):
                    if m == 0:
                        root()
                attention(UX, mix_hooks(UX))
                split_mix(TB - 1)
                normed_out(f"xo{e}")
                root()
                for m in range(KT):
                    renormed(m, f"ffn_pre{e}")
                gate_up(2 + e)
                down(2 + e, lambda m: publish_square(y_dn[:, m], m))
                root()

            for m, g in steps("ab_in"):
                if m == 0:
                    root()
                    exp_neg_abs(fw[:, 1], fw[:, 1])
                if m == 1:
                    act.wait_ge(act_in, n_.act_in.next())
                    A(cum_h[:], cum[:], ACT.Copy).then_inc(act_out, 1)
                    act.dma_start(sel[:], sel_dram).then_inc(sel_in, 16)
                if m == 8:
                    act.wait_ge(sel_in, 16)
                    A(sel_r[:], sel[:], ACT.Copy).then_inc(sel_ready, 1)
            for j in range(4):
                copy_values(v_tf[:, j], j)

            def split_conv(j):
                act.wait_ge(feat_in, j + 1)
                A(xh[:, 4 + j], conv_f[:, j], ACT.Copy).then_inc(feat_hi, 1)

            hooks = mix_hooks(UF, 4)
            for j in range(4):
                hooks.setdefault(4 + j, []).append(lambda j=j: split_conv(j))
            attention(UF, hooks)
            split_mix(TB - 1, 4)
            load_memory()
            publish_memory(0)
            normed_out("ab_out")
            memory_attention(0)
            for m in range(KT):
                renormed(m, "mix_pre1")

            for m, g in steps("c_u"):
                if m == 0:
                    root()
                act.wait_ge(u_conv, m + 1)
                A(u_h[:, m], u_r[:, m], ACT.Copy).then_inc(u_hi, 1)
            for n in range(4):
                c = CHUNK0["lru"] + n
                high(c + LEAD)
                act.wait_ge(chunk_done, c + 1)
                g = BANK0["lru"] + 4 * n
                for q, (dst, bias) in enumerate(((r_l, "ba"), (i_l, "bi"))):
                    for k in range(2):
                        A(dst[:, 2 * n + k], ps[:, (g + 2 * q + k) % 4], ACT.Sigmoid,
                          bias=col(bias, 2 * n + k)).then_inc(evac_done, 1)
            act.wait_ge(evac_done, BANK0["lru"] + 16)
            for m, g in steps("c_gate"):
                if m == 0:
                    for k in range(KT):
                        A(decay[:, k], r_l[:, k], ACT.Exp, scale=c8[:, k:k + 1])
                if m == 1:
                    for k in range(KT):
                        last = A(r_l[:, k], r_l[:, k], ACT.Tanh, scale=c4[:, k:k + 1])
                    last.then_inc(act_self, 1)
                if m == 2:
                    act.wait_ge(act_self, 1)
                    for k in range(KT):
                        A(r_l[:, k], r_l[:, k], ACT.Sqrt).then_inc(lru_act, 1)
                if m >= 3:
                    for k in range(m if m > 3 else 0, m + 1):
                        act.wait_ge(evac_done, BANK0["c_gate"] + k + 1)
                        A(gate_r[:, k], gate_r[:, k], ACT.Gelu_apprx_tanh).then_inc(gelu_done, 1)
                for k in STATES.get(m, ()):
                    act.wait_ge(feat_in, 4 + k + 1)
                    A(y_h[:, k], r_l[:, k], ACT.Copy).then_inc(feat_hi, 1)
            load_memory()
            publish_memory(1)
            normed_out("c_out")
            memory_attention(1)

        @block.vector
        def _(dve):
            n_ = Shared()
            V = nc.vector
            fp = lambda t: t.bitcast(f32)

            def mark(ins):
                ins.then_inc(dve_self, 1)
                return n_.dself.next()

            def link(ins):
                dve.wait_ge(dve_self, mark(ins))

            def accumulate(m, n=T):
                if m == 0:
                    return
                if m > 1:
                    dve.wait_ge(acc_ready, n_.acc.n)
                V.tensor_tensor(acc[:, 0:n], acc[:, 0:n], tmpa[:, m % 2, 0:n], ALU.add).then_inc(acc_ready, 1)
                n_.acc.next()

            def publish(m, name):
                dve.wait_ge(xh_ready, n_.xh.next())
                accumulate(m)
                V.scalar_tensor_tensor(out=xl[:, m], in0=x[:, m], scalar=gain(name, m),
                                       in1=fp(xh)[:, m], op0=ALU.mult,
                                       op1=ALU.subtract).then_inc(xl_ready, 1)

            def publish_square(m):
                dve.wait_ge(xh_ready, n_.xh.next())
                accumulate(m)

            def inverse_rms(dst, eps, n=T):
                dve.wait_ge(ss_done, n_.ss.next())
                V.tensor_scalar(tmpb[:, 0, 0:n], ps[:, MISC, 0:n], 1.0 / D, eps, ALU.mult,
                                ALU.add).then_inc(var_done, 1)
                dve.wait_ge(sd_done, n_.sd.next())
                link(V.reciprocal(dst[:, 0:n], tmpb[:, 0, 0:n]))

            def tiles(name):
                for m in range(TILES[name]):
                    dve.wait_ge(chunk_done, CHUNK0[name] + m + 1)
                    yield m, ps[:, (BANK0[name] + m) % 4, :]

            def scaled(dst, bank, n=T, r=rstd, rows=P):
                return V.tensor_tensor(dst, bank[0:rows, 0:n], r[0:rows, 0:n], ALU.mult)

            def rotate(dst, src, swapped):
                dve.wait_ge(swap_ready, n_.swap.next())
                V.tensor_tensor(swapped, swapped, rope[:, 1], ALU.mult)
                link(V.tensor_tensor(dst, src, rope[:, 0], ALU.mult))
                V.tensor_tensor(dst, dst, swapped, ALU.add).then_inc(proj_ready, 1)

            def magnitude(dst, src):
                return V.scalar_tensor_tensor(out=dst, in0=src, scalar=-1.0, in1=src, op0=ALU.mult,
                                              op1=ALU.max)

            def log1p_of(e, t, s, r):
                link(V.tensor_scalar(t, e, 2.0, None, ALU.add))
                link(V.reciprocal(r, t))
                link(V.tensor_tensor(s, e, r, ALU.mult))
                link(V.tensor_tensor(r, s, s, ALU.mult))
                link(V.tensor_scalar(t, r, 1.0 / (2 * ATANH_TERMS + 1), None, ALU.mult))
                for a in range(ATANH_TERMS - 1, 0, -1):
                    link(V.scalar_tensor_tensor(out=t, in0=t, scalar=1.0 / (2 * a + 1), in1=r,
                                                op0=ALU.add, op1=ALU.mult))
                link(V.tensor_scalar(t, t, 1.0, 2.0, ALU.add, ALU.mult))
                link(V.tensor_tensor(s, s, t, ALU.mult))

            def attention(units, hooks, mix):
                u0 = n_.units.n
                n_.units.n += len(units)
                pairs = len(units) // 2
                ended = {}
                for s in range(pairs + 2):
                    for a in range(2 * s, 2 * s + 2 if s < pairs else 0):
                        u, n = units[a], u0 + a
                        slot, h = n_.unit_groups.n % 4, u["index"]
                        dve.wait_ge(s_ready, n + 1)
                        if n >= 3:
                            dve.wait_ge(p_ready, n - 2)
                        start = 3.0e38 if u["sink"] is None else negsink[:, u["sink"]:u["sink"] + 1]
                        V.tensor_tensor_reduce(out=sm[:, n % 3, 0:u["nk"]],
                                               in0=ps[:, S_BANKS[n % 3], 0:u["nk"]], in1=u["mask"],
                                               scale=-u["scale"], scalar=start, op0=ALU.add,
                                               op1=ALU.min,
                                               accum_out=negm[:, slot, h:h + 1]).then_inc(sm_done, 1)
                        if u["last"]:
                            if u["sink"] is not None:
                                dve.wait_ge(sm_done, n + 1)
                                V.tensor_tensor(sinkarg[:, 0], negm[:, slot], col("sink", 0, 8),
                                                ALU.add).then_inc(sink_in, 1)
                            ended[s] = (n, slot, u["last"])
                            n_.unit_groups.next()
                    if 1 <= s <= pairs:
                        n = u0 + 2 * s - 2
                        nk = units[n - u0]["nk"]
                        dve.wait_ge(pt_ready, n + 1)
                        if n >= 3:
                            dve.wait_ge(o_done, n - 2)
                        V.tensor_copy(pt[:, n % 3, 0:nk],
                                      ps[:, PT_BANKS[n % 2], 0:nk]).then_inc(pt_copied[0], 1)
                    if s - 2 in ended:
                        n, slot, last = ended[s - 2]
                        dve.wait_ge(o_done, n + 1)
                        take_group(last, slot, mix)
                    for hook in hooks.get(s, []):
                        hook()

            group_no = Seq()

            def weighted(dst, weights_8, heads=8, width=HD):
                bank = ps[:, O_BANKS[(group_no.next() - 1) % 2], :]
                return V.tensor_tensor(dst, bank.rearrange("p (h d) -> p h d", h=heads),
                                       weights_8.rearrange("p (h o) -> p h o", o=1).broadcast_to(
                                           [P, heads, width]), ALU.mult)

            def take_group(last, slot, mix):
                _, kind, t, part = last
                heads = 2 if kind == "memory" else 8
                if kind == "B":
                    dve.wait_ge(sink_out, n_.sink.next())
                    link(V.tensor_tensor(den[:, slot], den[:, slot], sinkarg[:, 1], ALU.add))
                link(V.reciprocal(wgt[:, 0:heads], den[:, slot, 0:heads]))
                if kind in ("sel", "win"):
                    b = 1 if kind == "sel" else 2
                    gates = gate_t[:, t].rearrange("p (h b) -> p b h", b=3)[:, b]
                    link(V.tensor_tensor(wgt[:], wgt[:], gates, ALU.mult))
                    link(weighted(tmpa[:, 0].rearrange("p (h d) -> p h d", h=8), wgt[:]))
                    V.tensor_tensor(mix[:, t, 0:T], mix[:, t, 0:T], tmpa[:, 0], ALU.add).then_inc(o_free, 1)
                    dve.wait_ge(o_free, group_no.n)
                    return
                at = T if kind == "B" else part * T
                dst = mix[:, t, at:at + T].rearrange("p (h d) -> p h d", h=heads)
                weighted(dst, wgt[:, 0:heads], heads, T // heads).then_inc(o_free, 1)
                dve.wait_ge(o_free, group_no.n)

            def split_mix(t, blocks=8):
                for half in range(blocks // 4):
                    dve.wait_ge(mixh_ready, n_.mixh.next())
                    dst = (slice(None), slice(4 * half, 4 * half + 4), tokens(t))
                    V.tensor_tensor(xl[dst], ps[:, MISC, :].rearrange("p (f q) -> p f q", f=4),
                                    fp(xh)[dst], ALU.subtract).then_inc(mixl_ready, 1)

            def mix_hooks(units, blocks=8):
                per = len(units) // TB // 2
                return {t * per + LAG: [lambda t=t: split_mix(t - 1, blocks)] for t in range(1, TB)}

            def gate_up(f):
                name = f"gu{f}"
                c0, g0 = CHUNK0[name], BANK0[name]

                def pair(j, i):
                    for q, dst in ((0, tmpb), (1, tmpa)):
                        m = 2 * j + q
                        dve.wait_ge(chunk_done, chunk_at(c0 + m + 1, i, 4))
                        if i is None and m == 0:
                            inverse_rms(rstd, 1e-5 if f < 2 else 1e-6)
                        scaled(dst[:, j % 2], ps[:, (g0 + m) % 4, :]).then_inc(evac_done, 1)
                    dve.wait_ge(silu_ready, n_.silu.next())
                    V.tensor_tensor(tmpb[:, j % 2], tmpa[:, j % 2], tmpb[:, j % 2],
                                    ALU.mult).then_inc(prod_ready, 1)
                    dve.wait_ge(hh_ready, n_.hh.next())
                    at = (lambda t: t[:, j, :]) if i is None else \
                        (lambda t: t[:, bass.ds(i * 2 + j, 1), :].rearrange("p a t -> p (a t)"))
                    V.tensor_tensor(at(hl), tmpb[:, j % 2], at(fp(hh)), ALU.subtract).then_inc(hl_ready, 1)

                pair(0, None)
                pair(1, None)
                with dve.Fori(1, FJ // 2) as i:
                    n_.silu.enter(i, 1, 2)
                    n_.hh.enter(i, 1, 2)
                    pair(0, i)
                    pair(1, i)
                n_.silu.leave(FJ // 2 - 1)
                n_.hh.leave(FJ // 2 - 1)

            def down(f, evac, then):
                for m in range(KT):
                    dve.wait_ge(chunk_done, CHUNK0[f"dn{f}"] + DN_CHUNKS * (m + 1))
                    evac(m, ps[:, (BANK0[f"dn{f}"] + m) % 4, :]).then_inc(evac_done, 1)
                    if m:
                        then(m - 1)
                then(KT - 1)

            def residual(m, bank):
                return V.tensor_tensor(x[:, m], bank, x[:, m], ALU.add)

            def residual_out(name, gname):
                for m, bank in tiles(name):
                    residual(m, bank).then_inc(evac_done, 1)
                for m in range(KT):
                    publish(m, gname)

            dve.wait_ge(small_in_sem, 16)
            V.tensor_scalar(negsink[:], col("sink", 0, 8), -1.0, None, ALU.mult)
            magnitude(lp[:, 0], col("lam", 0, 8)).then_inc(act_in, 1)
            dve.wait_ge(act_out, n_.act_out.next())
            log1p_of(lp[:, 1], lp[:, 0], lp[:, 2], lp[:, 3])
            link(V.tensor_scalar(lp[:, 0], col("lam", 0, 8), -1.0, 0.0, ALU.mult, ALU.max))
            link(V.tensor_tensor(lp[:, 0], lp[:, 0], lp[:, 2], ALU.add))
            V.tensor_scalar(c4[:], lp[:, 0], 4.0, None, ALU.mult)
            link(V.tensor_scalar(c8[:], lp[:, 0], -8.0, None, ALU.mult))

            for m in range(KT):
                publish(m, "attn0")
            dve.wait_ge(const_in, CONST_DMAS * 16)
            pending = None
            for m, bank in tiles("in_e"):
                if m == 0:
                    inverse_rms(rstd, 1e-5)
                dst = (z_c[:, m] if m < 2 else z_v0[:, m - 2] if m < 5 else rot0[:, m % 2, 0] if m < 8
                       else q_p0[:, m - 8] if m < 12 else rot0[:, m % 2, 0] if m < 16 else gate_f[:])
                scaled(dst, bank).then_inc(evac_done, 1)
                if m in (1, 3):
                    kv = m // 2
                    dve.wait_ge(blk_copied, kv + 1)
                    pe_cols = col("pe", 16 * kv, 16 * kv + 16).rearrange("p (r o) -> p r o", o=1)
                    V.tensor_tensor(blk[:], blk[:], pe_cols.broadcast_to([P, 16, 62]),
                                    ALU.add).then_inc(blk_added, 1)
                if m in (2, 4):
                    kv = m // 2 - 1
                    dve.wait_ge(blk_hi, kv + 1)
                    V.tensor_tensor(blk_l[:, kv], blk[:], fp(blk_h)[:, kv], ALU.subtract).then_inc(cmp_blk, 1)
                if pending:
                    rotate(*pending)
                    pending = None
                if 5 <= m < 16:
                    out_tile = k_r0[:, m - 5] if m < 8 else q_r0[:, m - 8]
                    pending = (out_tile, dst, rot0[:, m % 2, 1])
                else:
                    dve.wait_ge(evac_done, BANK0["in_e"] + m + 1)
                    V.engine_nop().then_inc(proj_ready, 1)
            for m in range(4):
                dve.wait_ge(chunk_done, CHUNK0["cmp"] + 2 * m + 2)
                V.tensor_copy(hid[:, m // 2, m % 2], ps[:, (BANK0["cmp"] + m) % 4, 0:62]).then_inc(evac_done, 1)
                dve.wait_ge(evac_done, BANK0["cmp"] + m + 1)
                V.engine_nop().then_inc(cmp_hid, 1)
            dve.wait_ge(cmp_ps, 2)
            V.memset(v_diag[:], 0.0)
            link(V.memset(kc_t[:], 0.0))
            for g in range(2):
                rows = slice(g * HD, (g + 1) * HD)
                V.tensor_copy(kc_t[rows, 0:31], ps[rows, MISC, g * 31:(g + 1) * 31])
                for q in range(4):
                    last = V.tensor_copy(v_diag[32 * q:32 * q + 31, g, q],
                                         ps[0:31, MISC, 128 + g * HD:128 + (g + 1) * HD])
            last.then_inc(cmp_vk, 1)

            def cmp_softmax(t):
                dve.wait_ge(cmp_ps, 3 + 3 * t)
                scores = ps[:, MISC, 0:256].rearrange("p (h c) -> p h c", h=8)
                mask = cmask[:, t].rearrange("p (o c) -> p o c", o=1).broadcast_to([P, 8, 32])
                link(V.tensor_tensor(s_c[:], scores, mask, ALU.add))
                link(V.tensor_reduce(cst[:, 0], s_c[:], AX.X, ALU.max))
                link(V.tensor_scalar(cst[:, 0], cst[:, 0], -1.0e20, None, ALU.max))
                V.tensor_tensor(s_c[:], s_c[:], cst[:, 0].rearrange("p (h o) -> p h o", o=1)
                                .broadcast_to([P, 8, 32]), ALU.subtract).then_inc(cmp_masked, 1)
                dve.wait_ge(cmp_sb, 3 + 2 * t)
                link(V.tensor_reduce(cst[:, 1], s_c[:], AX.X, ALU.add))
                link(V.tensor_scalar(cst[:, 1], cst[:, 1], 1.0e-30, None, ALU.max))
                link(V.reciprocal(cst[:, 1], cst[:, 1]))
                gates = gate_t[:, t].rearrange("p (h b) -> p b h", b=3)[:, 0]
                link(V.tensor_tensor(cst[:, 1], cst[:, 1], gates, ALU.mult))

            def cmp_take(t):
                dve.wait_ge(cmp_ps, 5 + 3 * t)
                weighted(mix0[:, t, 0:T].rearrange("p (h d) -> p h d", h=8), cst[:, 1]).then_inc(o_free, 1)
                dve.wait_ge(o_free, group_no.n)

            hooks = mix_hooks(U0)
            for t in range(TB):
                if t:
                    hooks.setdefault(12 * t - 2, []).append(lambda t=t: cmp_softmax(t))
                hooks.setdefault(12 * t + 1, []).insert(0, lambda t=t: cmp_take(t))
            cmp_softmax(0)
            attention(U0, hooks, mix0)
            split_mix(TB - 1)
            residual_out("out_e", "ffn0")
            gate_up(0)
            down(0, residual, lambda m: publish(m, "attn1"))

            pending = None
            for m, bank in tiles("qkv"):
                if m == 0:
                    inverse_rms(rstd, 1e-5)
                if m < 8:
                    scaled(z_v1[:, m], bank).then_inc(evac_done, 1)
                    dve.wait_ge(evac_done, BANK0["qkv"] + m + 1)
                    V.engine_nop().then_inc(proj_ready, 1)
                    continue
                scaled(rot1[:, m % 2, 0], bank).then_inc(evac_done, 1)
                if pending:
                    rotate(*pending)
                pending = (q_r1[:, m - 8] if m < 16 else k_r1[:, m - 16], rot1[:, m % 2, 0], rot1[:, m % 2, 1])
            rotate(*pending)
            dve.wait_ge(tab_in, 16)
            attention(U1, mix_hooks(U1), mix1)
            split_mix(TB - 1)
            residual_out("out_o", "ffn1")
            gate_up(1)
            down(1, residual, publish_square)

            def x_updated(ins):
                ins.then_inc(x_ready, 1)
                n_.x.next()

            inverse_rms(rstd, 1e-5)
            for m in range(KT):
                x_updated(V.scalar_tensor_tensor(out=x[:, m], in0=x[:, m], scalar=gain("final", m),
                                                 in1=rstd[:], op0=ALU.mult, op1=ALU.mult))
                if m:
                    publish(m - 1, "mix_pre0")
            publish(KT - 1, "mix_pre0")

            def copy_out(y):
                return lambda m, bank: V.tensor_copy(y[:, m], bank)

            def add_normed(y, name, m):
                link(V.tensor_tensor(y[:, m], y[:, m], rstd[:], ALU.mult))
                x_updated(V.scalar_tensor_tensor(out=x[:, m], in0=y[:, m], scalar=gain(name, m),
                                                 in1=x[:, m], op0=ALU.mult, op1=ALU.add))

            def normed_out(name):
                for m, bank in tiles(name):
                    if m == 0 and name in ("ab_out", "c_out"):
                        inverse_rms(rstd_m, 1e-6, MEM)
                    copy_out(y_mid)(m, bank).then_inc(evac_done, 1)
                    if m:
                        publish_square(m - 1)
                publish_square(KT - 1)

            def publish_memory(e):
                for m in range(KT):
                    dve.wait_ge(mem_hi, n_.memh.next())
                    accumulate(m, MEM)
                    V.scalar_tensor_tensor(out=mem_l[:, m], in0=mem[:, m], scalar=gain(f"mem{e}", m),
                                           in1=fp(mem_h)[:, m], op0=ALU.mult,
                                           op1=ALU.subtract).then_inc(mem_ready, 1)

            def memory_attention(e):
                for m, bank in tiles(f"xkv{e}"):
                    if m == 0:
                        inverse_rms(rstd, 1e-6)
                    scaled(k_x[:, m] if m < 8 else z_vx[:, m - 8], bank, MEM, rstd_m).then_inc(evac_done, 1)
                    if m < KT:
                        add_normed(y_mid, f"mix_post{e}", m)
                    dve.wait_ge(evac_done, BANK0[f"xkv{e}"] + m + 1)
                    V.engine_nop().then_inc(proj_ready, 1)
                    if 1 <= m <= KT:
                        publish(m - 1, f"cross_pre{e}")
                for m, bank in tiles(f"xq{e}"):
                    if m == 0:
                        inverse_rms(rstd, 1e-6)
                    scaled(q_x[:, m], bank).then_inc(evac_done, 1)
                    dve.wait_ge(evac_done, BANK0[f"xq{e}"] + m + 1)
                    V.engine_nop().then_inc(proj_ready, 1)
                attention(UX, mix_hooks(UX), mix_x)
                split_mix(TB - 1)
                normed_out(f"xo{e}")
                inverse_rms(rstd, 1e-6)
                for m in range(KT):
                    add_normed(y_mid, f"cross_post{e}", m)
                    if m:
                        publish(m - 1, f"ffn_pre{e}")
                publish(KT - 1, f"ffn_pre{e}")
                gate_up(2 + e)
                down(2 + e, copy_out(y_dn), publish_square)
                inverse_rms(rstd, 1e-6)
                for m in range(KT):
                    add_normed(y_dn, f"ffn_post{e}", m)
                    if m and not e:
                        publish(m - 1, "mix_pre1")
                if not e:
                    publish(KT - 1, "mix_pre1")

            for m, bank in tiles("ab_in"):
                if m == 0:
                    inverse_rms(rstd, 1e-6)
                    link(scaled(fw[:, 0], bank, rows=8))
                    link(V.tensor_scalar(fw[:, 0], fw[:, 0], small[0:8, SMALL["bf"]], None, ALU.add))
                    magnitude(fw[:, 1], fw[:, 0]).then_inc(act_in, 1)
                    dve.wait_ge(act_out, n_.act_out.next())
                    log1p_of(fw[:, 1], fw[:, 2], fw[:, 3], cum[:])
                    link(V.tensor_scalar(fw[:, 0], fw[:, 0], 0.0, None, ALU.min))
                    link(V.tensor_scalar(fw[:, 3], fw[:, 3], -1.0, None, ALU.mult))
                    link(V.tensor_tensor_scan(out=cum[:], data0=fw[:, 0], data1=fw[:, 3], initial=0.0,
                                              op0=ALU.add, op1=ALU.add))
                    V.engine_nop().then_inc(evac_done, 1)
                    V.engine_nop().then_inc(act_in, 1)
                    V.memset(gated[:, :, 0:2], 0.0).then_inc(proj_ready, 1)
                    continue
                if m == 1:
                    dve.wait_ge(act_out, n_.act_out.next())
                    V.tensor_tensor(cum_l[:], cum[:], fp(cum_h)[:], ALU.subtract).then_inc(cum_ready, 1)
                j = (m - 1) % 4
                kind = ("v", "q", "k", "c", "u", "b")[(m - 1) // 4]
                if kind in "vqk":
                    scaled({"v": z_vf, "q": q_f, "k": k_f}[kind][:, j], bank).then_inc(evac_done, 1)
                elif kind == "c":
                    scaled(gated[:, j, 2:2 + T], bank).then_inc(evac_done, 1)
                else:
                    scaled(tmpb[:, m % 2], bank).then_inc(evac_done, 1)
                dve.wait_ge(evac_done, BANK0["ab_in"] + m + 1)
                w = lambda a: col("abconv", 3 * j + a)
                if kind == "u":
                    link(V.tensor_tensor(gated[:, j, 2:2 + T], gated[:, j, 2:2 + T], tmpb[:, m % 2], ALU.mult))
                    link(V.tensor_scalar(conv_f[:, j], gated[:, j, 2:2 + T], w(2), None, ALU.mult))
                    for a in (1, 0):
                        ins = V.scalar_tensor_tensor(out=conv_f[:, j], in0=gated[:, j, a:a + T], scalar=w(a),
                                                     in1=conv_f[:, j], op0=ALU.mult, op1=ALU.add)
                        if a:
                            link(ins)
                    ins.then_inc(proj_ready, 1)
                elif kind == "b":
                    dve.wait_ge(proj_ready, PROJ_AB + m)
                    V.tensor_tensor(conv_f[:, j], conv_f[:, j], tmpb[:, m % 2], ALU.mult).then_inc(feat_in, 1)
                    V.engine_nop().then_inc(proj_ready, 1)
                else:
                    V.engine_nop().then_inc(proj_ready, 1)

            def split_conv(j):
                dve.wait_ge(feat_hi, j + 1)
                V.tensor_tensor(xl[:, 4 + j], conv_f[:, j], fp(xh)[:, 4 + j], ALU.subtract).then_inc(feat_ready, 1)

            dve.wait_ge(tab_in, 32)
            hooks = mix_hooks(UF, 4)
            for j in range(4):
                hooks.setdefault(4 + j, []).append(lambda j=j: split_conv(j))
            attention(UF, hooks, mix_f)
            split_mix(TB - 1, 4)
            publish_memory(0)
            normed_out("ab_out")
            memory_attention(0)

            link(V.memset(z_u[:, :, 0:3], 0.0))
            for m, bank in tiles("c_u"):
                if m == 0:
                    inverse_rms(rstd, 1e-6)
                z = z_u[:, m % 2]
                scaled(z[:, 3:3 + T], bank).then_inc(evac_done, 1)
                dve.wait_ge(evac_done, BANK0["c_u"] + m + 1)
                w = lambda a: col("cconv", 4 * m + a)
                link(V.tensor_scalar(u_r[:, m], z[:, 3:3 + T], w(3), col("cbias", m), ALU.mult, ALU.add))
                for a in (2, 1, 0):
                    ins = V.scalar_tensor_tensor(out=u_r[:, m], in0=z[:, a:a + T], scalar=w(a),
                                                 in1=u_r[:, m], op0=ALU.mult, op1=ALU.add)
                    if a:
                        link(ins)
                ins.then_inc(u_conv, 1)
                dve.wait_ge(u_hi, m + 1)
                V.tensor_tensor(u_l[:, m], u_r[:, m], fp(u_h)[:, m], ALU.subtract).then_inc(proj_ready, 1)
            for n in range(4):
                for k in range(2 * n, 2 * n + 2):
                    dve.wait_ge(evac_done, BANK0["lru"] + 2 * n + 3 + k)
                    iu = mark(V.tensor_tensor(u_r[:, k], u_r[:, k], i_l[:, k], ALU.mult))
            dve.wait_ge(dve_self, iu)

            def state_low(k):
                dve.wait_ge(feat_hi, 4 + k + 1)
                V.tensor_tensor(y_l[:, k], r_l[:, k], fp(y_h)[:, k], ALU.subtract).then_inc(feat_ready, 1)

            def state(k):
                b, y = tmpb[:, k % 2], r_l[:, k]
                dve.wait_ge(lru_act, k + 1)
                link(V.scalar_tensor_tensor(out=b, in0=decay[:, k], scalar=1.0, in1=r_l[:, k], op0=ALU.add,
                                            op1=ALU.mult))
                link(V.tensor_tensor(b, b, u_r[:, k], ALU.mult))
                link(V.tensor_tensor_scan(out=y, data0=decay[:, k], data1=b, initial=0.0, op0=ALU.mult,
                                          op1=ALU.add))
                dve.wait_ge(gelu_done, k + 1)
                V.tensor_tensor(y, y, gate_r[:, k], ALU.mult).then_inc(feat_in, 1)
                if k:
                    state_low(k - 1)

            for m, bank in tiles("c_gate"):
                scaled(gate_r[:, m], bank).then_inc(evac_done, 1)
                for k in STATES.get(m, ()):
                    state(k)
            state_low(KT - 1)
            publish_memory(1)
            normed_out("c_out")
            memory_attention(1)


def _tables():
    p = np.arange(P)[:, None]
    rel = np.arange(T)[None, :] - (T - P)
    dist = p - rel
    causal = np.where(dist >= 0, 0.0, NEG)
    rel2 = np.arange(2 * P)[None, :] - P
    window = np.where((p - rel2 >= 0) & (p - rel2 < P), 0.0, NEG)
    count = ((dist >= 0) & (dist <= 128)).astype(int) + ((dist >= 0) & (dist % 4 == 0)) \
        + ((dist >= 0) & (dist % 16 == 0))
    many = np.where(count > 0, np.log(np.maximum(count, 1)) / SCALE, NEG)
    return np.concatenate([np.eye(P), causal, window, many], axis=1).astype(np.float32)


def _rope():
    inv = np.float32(1.0) / (np.float32(10000.0) ** (np.arange(0, HD, 2, dtype=np.float32) / np.float32(HD)))
    ang = (np.arange(T, dtype=np.float32)[:, None] * inv[None, :]).astype(np.float32)
    cos, sin = np.cos(ang).T, np.sin(ang).T
    one = np.stack([np.concatenate([cos, cos]), np.concatenate([-sin, sin])], axis=1)
    return np.concatenate([one, one], axis=0).astype(np.float32)


def _cmp_mask():
    q = np.arange(T).reshape(TB, P).T[:, :, None]
    c = np.arange(32)[None, None, :]
    return np.where((16 * c + 31 <= q) & (c < NC_CMP), 0.0, NEG).astype(np.float32)


def _sel():
    s = np.zeros((8, 8, P), np.float32)
    s[np.arange(8), np.arange(8)] = -1.0 / SCALE
    return s


def _weight_tiles(w):
    k, m = w.shape
    if m % P:
        w = np.concatenate([w, np.zeros((k, -m % P), w.dtype)], axis=1)
    return w.reshape(k // P, P, -1, P).transpose(2, 1, 0, 3)


def _chunks(w):
    t = _weight_tiles(w)
    pad = -t.shape[2] % CT
    if pad:
        t = np.concatenate([t, np.zeros(t.shape[:2] + (pad, P), t.dtype)], axis=2)
    m, p, k, c = t.shape
    return t.reshape(m, p, k // CT, CT * c).transpose(0, 2, 1, 3).reshape(-1, P, CW)


def _cols(w, *widths_at):
    return np.concatenate([w[:, a:b] for a, b in widths_at], axis=1)


def _stream(v):
    e = v["w_in_e"][0]
    part = lambda n: (512 + 128 * n, 640 + 128 * n)
    pairs = lambda base: [(base + 64 * h, base + 64 * h + 64) for j in range(4) for h in (j, j + 4)]
    bq = 512 + 768 + 24
    in_e = _cols(e, part(0), part(1), part(3), part(5), (bq + 640, bq + 768), part(2), part(4),
                 (bq + 512, bq + 640), *pairs(0), *pairs(bq), (1280, 1304))
    ff = lambda w: w.reshape(D, 2, FJ, P)[:, ::-1].transpose(0, 2, 1, 3).reshape(D, 2 * FF)
    ab = v["ab_w_in_2"][0]
    qkv = v["w_qkv_o"][0]

    def lru():
        a, i = v["c_w_a_2"][0], v["c_w_i_2"][0]
        return np.concatenate([
            np.concatenate([_weight_tiles(w[n]).transpose(1, 0, 2, 3).reshape(P, 4 * P) for w in (a, i)],
                           axis=1)[None] for n in range(4)])

    parts = [
        _chunks(in_e), _chunks(v["cmp_k_w1"][0]), _chunks(v["cmp_v_w1"][0]), _chunks(v["w_out_e"][0]),
        _chunks(ff(v["w_gate_up"][0])), _chunks(v["w_down"][0]),
        _chunks(_cols(qkv, (2048, 3072), (0, 2048))), _chunks(v["w_out_o"][0]),
        _chunks(ff(v["w_gate_up"][1])), _chunks(v["w_down"][1]),
        _chunks(_cols(ab, (1536, 1544))),
        _chunks(_cols(ab, (1024, 1536), (0, 1024), (2056, 3080), (1544, 2056))),
        _chunks(v["ab_w_out_2"][0])]
    for i in range(2):
        if i:
            c_in = v["c_w_in_2"][0]
            parts += [_chunks(c_in[:, 1024:]), lru(), _chunks(c_in[:, :1024]),
                      _chunks(v["c_w_out_2"][0])]
        parts += [_chunks(v["w_xkv_2"][i]), _chunks(v["w_xq_2"][i]), _chunks(v["w_xo_2"][i]),
                  _chunks(ff(v["w_ffn_gu_2"][i])), _chunks(v["w_ffn_down_2"][i])]
    return np.concatenate(parts, axis=0)


def _small(v):
    vec = lambda a: a.reshape(-1, P).T
    gains = [v["attn_norm"][0], v["ffn_norm"][0], v["attn_norm"][1], v["ffn_norm"][1], v["final_norm"]]
    for i in range(2):
        gains += [v[f"g_{n}_2"][i] for n in ("mix_pre", "mix_post", "cross_pre", "mem", "cross_post",
                                             "ffn_pre", "ffn_post")]
    w2 = lambda w: w.reshape(2, P, HD).transpose(1, 0, 2)
    pe = lambda a: a[0].reshape(16, P).T
    bf = np.zeros((P, 1), np.float32)
    bf[0:8, 0] = v["ab_b_f_2"][0]
    taps = lambda w: w.T.reshape(-1, P, w.shape[0]).transpose(1, 0, 2).reshape(P, -1)
    k2 = w2(v["cmp_k_w2"][0])
    return np.concatenate(
        [vec(g) for g in gains] +
        [np.broadcast_to(v["sinks"][0], (P, 8)), pe(v["cmp_pe_k"]), pe(v["cmp_pe_v"]),
         w2(v["cmp_v_w2"][0]).reshape(P, -1), np.concatenate([k2, k2], axis=2).reshape(P, -1),
         taps(v["ab_conv_w_2"][0]), taps(v["c_conv_w_2"][0]), vec(v["c_conv_b_2"][0]),
         vec(v["c_b_a_2"][0]), vec(v["c_b_i_2"][0]), vec(v["c_lam_2"][0]), bf], axis=1)


def kernel(**inputs):
    import concourse.bacc as bacc
    from concourse.bass_utils import run_bass_kernel_spmd

    v = {n: np.asarray(a) for n, a in inputs.items()}
    feature_major = lambda a: np.ascontiguousarray(a.T.reshape(KT, P, -1).transpose(1, 0, 2))
    arrays = {
        "x_in": feature_major(v["x"][0]), "mem_in": feature_major(v["mem_2"][0]),
        "weights_in": _stream(v), "small_in": np.ascontiguousarray(_small(v)),
        "tables_in": _tables(), "rope_in": _rope(), "cmp_mask_in": _cmp_mask(), "sel_in_dram": _sel(),
    }
    nc = bacc.Bacc("TRN2", target_bir_lowering=False, num_devices=1)
    aps = [nc.dram_tensor(n, a.shape, mybir.dt.from_np(a.dtype), kind="ExternalInput").ap()
           for n, a in arrays.items()]
    out = nc.dram_tensor("x_out", (P, KT, T), mybir.dt.float32, kind="ExternalOutput").ap()
    two_stacks(nc, *aps, out)
    r = run_bass_kernel_spmd(nc, [arrays], core_ids=[0])
    return r.results[0]["x_out"].transpose(1, 0, 2).reshape(D, T).T[None]
```
